# Optimizing a Trainium2 kernel written in Bass

```python
import jax, jax.numpy as jnp
from jax import lax
import numpy as np

D_MODEL = 1024
BATCH = 1
SEQ = 1024
DEPTH = 2
DEC_BATCH = 8
DEC_SEQ = 4
PAST_LEN = 4096
PAGE_SIZE = 128

N_HEADS = 8
HEAD_DIM = 64
N_KV_HEADS = 2
GROUP = N_HEADS // N_KV_HEADS
ATTN_W = N_HEADS * HEAD_DIM
KV_W = N_KV_HEADS * HEAD_DIM
CONV_W = D_MODEL - ATTN_W
CONV_K = 3
WINDOW = 128
BLOCK = 128
W_BUF = min(WINDOW, PAST_LEN)
ROPE_THETA = 10000.0
PLE_DIM = 256
EPS = 1e-6
SCALE = HEAD_DIM ** -0.5
NEG = -1e30
IN_W = 2 * ATTN_W + 2 * KV_W + 4 * CONV_W
SPLITS = (ATTN_W, ATTN_W + KV_W, ATTN_W + 2 * KV_W, 2 * ATTN_W + 2 * KV_W,
          2 * ATTN_W + 2 * KV_W + CONV_W, 2 * ATTN_W + 2 * KV_W + 2 * CONV_W,
          2 * ATTN_W + 2 * KV_W + 3 * CONV_W)

kernel_name = "hymba_swa_sink_shortconv_ple_step"

def rmsnorm(x, g):
    xf = x.astype(jnp.float32)
    r = lax.rsqrt(jnp.mean(xf * xf, axis=-1, keepdims=True) + EPS)
    return (xf * r).astype(x.dtype) * g

def rope(x, pos):
    inv = ROPE_THETA ** (-jnp.arange(0, HEAD_DIM, 2, dtype=jnp.float32) / HEAD_DIM)
    ang = pos[:, None] * inv[None, :]
    cos = jnp.concatenate([jnp.cos(ang), jnp.cos(ang)], -1)[None, :, None, :].astype(x.dtype)
    sin = jnp.concatenate([jnp.sin(ang), jnp.sin(ang)], -1)[None, :, None, :].astype(x.dtype)
    x1, x2 = jnp.split(x, 2, axis=-1)
    return x * cos + jnp.concatenate([-x2, x1], -1) * sin

def sink_softmax(s, sink):
    m = jnp.maximum(jnp.max(s, axis=-1, keepdims=True), sink)
    e = jnp.exp(s - m)
    return e / (jnp.sum(e, axis=-1, keepdims=True) + jnp.exp(sink - m))

def branch_inputs(x, g_norm, w_in, pos):
    b, t = x.shape[0], x.shape[1]
    z = rmsnorm(x, g_norm) @ w_in
    q, k, v, ga, bg, cg, hc, gc = jnp.split(z, SPLITS, axis=-1)
    q = rope(q.reshape(b, t, N_HEADS, HEAD_DIM), pos)
    k = rope(k.reshape(b, t, N_KV_HEADS, HEAD_DIM), pos)
    v = v.reshape(b, t, N_KV_HEADS, HEAD_DIM)
    return q, k, v, ga, bg, cg * hc, gc

def attn_prompt(q, k, v, sink):
    b, s_len = q.shape[0], q.shape[1]
    nb = s_len // BLOCK
    qb = q.reshape(b, nb, BLOCK, N_KV_HEADS, GROUP, HEAD_DIM)

    def with_prev(t):
        tb = t.reshape(b, nb, BLOCK, N_KV_HEADS, HEAD_DIM)
        prev = jnp.pad(tb[:, :-1], ((0, 0), (1, 0), (0, 0), (0, 0), (0, 0)))
        return jnp.concatenate([prev, tb], axis=2)

    kk, vv = with_prev(k), with_prev(v)
    s = jnp.einsum('bnqhgd,bnkhd->bnhgqk', qb, kk, preferred_element_type=jnp.float32) * SCALE
    qi = jnp.arange(BLOCK)[:, None]
    kj = jnp.arange(2 * BLOCK)[None, :]
    diff = BLOCK + qi - kj
    blk = jnp.arange(nb)[:, None, None]
    valid = (diff >= 0) & (diff < WINDOW) & (blk * BLOCK - BLOCK + kj >= 0)
    s = jnp.where(valid[None, :, None, None], s, NEG)
    p = sink_softmax(s, sink.astype(jnp.float32).reshape(1, 1, N_KV_HEADS, GROUP, 1, 1))
    o = jnp.einsum('bnhgqk,bnkhd->bnqhgd', p.astype(vv.dtype), vv)
    return o.reshape(b, s_len, ATTN_W)

def attn_sample(q, k, v, kbuf, vbuf, sink):
    b, t = q.shape[0], q.shape[1]
    kk = jnp.concatenate([kbuf, k], axis=1)
    vv = jnp.concatenate([vbuf, v], axis=1)
    qpos = PAST_LEN + jnp.arange(t)
    kpos = jnp.concatenate([PAST_LEN - W_BUF + jnp.arange(W_BUF), qpos])
    diff = qpos[:, None] - kpos[None, :]
    valid = (diff >= 0) & (diff < WINDOW)
    qg = q.reshape(b, t, N_KV_HEADS, GROUP, HEAD_DIM)
    s = jnp.einsum('bqhgd,bkhd->bhgqk', qg, kk, preferred_element_type=jnp.float32) * SCALE
    s = jnp.where(valid[None, None, None], s, NEG)
    p = sink_softmax(s, sink.astype(jnp.float32).reshape(1, N_KV_HEADS, GROUP, 1, 1))
    o = jnp.einsum('bhgqk,bkhd->bqhgd', p.astype(vv.dtype), vv)
    return o.reshape(b, t, ATTN_W), kk[:, -W_BUF:], vv[:, -W_BUF:]

def causal_conv(u_pad, w, t):
    y = w[0] * u_pad[:, 0:t]
    for j in range(1, CONV_K):
        y = y + w[j] * u_pad[:, j:j + t]
    return y

def branch_output(x, o_attn, ga, bg, conv_out, gc, w_out, p_i, w_pg, w_pp):
    mix = jnp.concatenate([o_attn * jax.nn.silu(ga), bg * conv_out * jax.nn.silu(gc)], axis=-1)
    x = x + mix @ w_out
    return x + jax.nn.sigmoid(x @ w_pg) * (p_i @ w_pp)

def setup_inputs(seed: int = 0) -> dict:
    key = jax.random.key(seed)
    ks = jax.random.split(key, 18)
    f32 = jnp.float32
    n = lambda k, s, sc: jax.random.normal(k, s, f32) * sc
    return {
        "x_prompt": n(ks[0], (BATCH, SEQ, D_MODEL), 1.0),
        "x_sample": n(ks[1], (DEC_BATCH, DEC_SEQ, D_MODEL), 1.0),
        "cache_k": n(ks[2], (DEPTH, DEC_BATCH, W_BUF, N_KV_HEADS, HEAD_DIM), 1.0),
        "cache_v": n(ks[3], (DEPTH, DEC_BATCH, W_BUF, N_KV_HEADS, HEAD_DIM), 1.0),
        "state_conv": n(ks[4], (DEPTH, DEC_BATCH, CONV_K - 1, CONV_W), 1.0),
        "p_prompt": n(ks[5], (DEPTH, BATCH, SEQ, PLE_DIM), 1.0),
        "p_sample": n(ks[6], (DEPTH, DEC_BATCH, DEC_SEQ, PLE_DIM), 1.0),
        "g_norm": 1.0 + n(ks[7], (DEPTH, D_MODEL), 0.05),
        "w_in": n(ks[8], (DEPTH, D_MODEL, IN_W), D_MODEL ** -0.5),
        "sinks": n(ks[9], (DEPTH, N_HEADS), 0.5),
        "conv_w": n(ks[10], (DEPTH, CONV_K, CONV_W), CONV_K ** -0.5),
        "w_out": n(ks[11], (DEPTH, D_MODEL, D_MODEL), D_MODEL ** -0.5),
        "w_pg": n(ks[12], (DEPTH, D_MODEL, D_MODEL), D_MODEL ** -0.5),
        "w_pp": n(ks[13], (DEPTH, PLE_DIM, D_MODEL), PLE_DIM ** -0.5),
        "g_final": 1.0 + n(ks[14], (D_MODEL,), 0.05),
    }

def reference(x_prompt, x_sample, cache_k, cache_v, state_conv, p_prompt, p_sample,
              g_norm, w_in, sinks, conv_w, w_out, w_pg, w_pp, g_final):
    pos_p = jnp.arange(SEQ, dtype=jnp.float32)
    pos_s = PAST_LEN + jnp.arange(DEC_SEQ, dtype=jnp.float32)
    xp, xs = x_prompt, x_sample
    nkp, nvp, ncp, nks, nvs, ncs = [], [], [], [], [], []
    for i in range(DEPTH):
        q, k, v, ga, bg, u, gc = branch_inputs(xp, g_norm[i], w_in[i], pos_p)
        oa = attn_prompt(q, k, v, sinks[i])
        u_pad = jnp.pad(u, ((0, 0), (CONV_K - 1, 0), (0, 0)))
        yc = causal_conv(u_pad, conv_w[i], SEQ)
        xp = branch_output(xp, oa, ga, bg, yc, gc, w_out[i], p_prompt[i], w_pg[i], w_pp[i])
        nkp.append(k[:, SEQ - W_BUF:])
        nvp.append(v[:, SEQ - W_BUF:])
        ncp.append(u[:, SEQ - (CONV_K - 1):])
        q, k, v, ga, bg, u, gc = branch_inputs(xs, g_norm[i], w_in[i], pos_s)
        oa, kb, vb = attn_sample(q, k, v, cache_k[i], cache_v[i], sinks[i])
        u_pad = jnp.concatenate([state_conv[i], u], axis=1)
        yc = causal_conv(u_pad, conv_w[i], DEC_SEQ)
        xs = branch_output(xs, oa, ga, bg, yc, gc, w_out[i], p_sample[i], w_pg[i], w_pp[i])
        nks.append(kb)
        nvs.append(vb)
        ncs.append(u_pad[:, -(CONV_K - 1):])
    y_prompt = rmsnorm(xp, g_final)
    y_sample = rmsnorm(xs, g_final)
    return (y_prompt, y_sample, jnp.stack(nkp), jnp.stack(nvp), jnp.stack(ncp),
            jnp.stack(nks), jnp.stack(nvs), jnp.stack(ncs))


_drawn_inputs = setup_inputs


def setup_inputs(seed=0):
    import zlib

    import numpy as np

    out = dict(_drawn_inputs(seed))
    spreads = {}
    factors = {'sinks': 8.0}
    for name, (base, spread) in spreads.items():
        noise = np.random.default_rng([zlib.crc32(name.encode()), seed]).standard_normal(out[name].shape)
        drawn = base * np.exp(spread * noise) if base else spread * noise
        out[name] = __import__('jax').numpy.asarray(drawn.astype(out[name].dtype))
    for name, factor in factors.items():
        out[name] = (out[name] * factor).astype(out[name].dtype)
    return out
```

```python
from contextlib import ExitStack

import concourse.bass as bass
from concourse import mybir

F32 = mybir.dt.float32
F32R = mybir.dt.float32r
U32 = mybir.dt.uint32
ALU = mybir.AluOpType
ACT = mybir.ActivationFunctionType
AX = mybir.AxisListType
P = 128
NEG = -1e30
EPS = 1e-6


def hybrid_trunk(nc, x_prompt, x_sample, cache_k, cache_v, state_conv, p_prompt, p_sample, g_norm, w_in,
                 sinks, conv_w, w_out, w_pg, w_pp, g_final, rope_cos, rope_sin, decode_mask,
                 y_prompt, y_sample, new_k_prompt, new_v_prompt, new_conv_prompt,
                 new_k_sample, new_v_sample, new_conv_sample):
    DEPTH, D = g_norm.shape
    SEQ = x_prompt.shape[1]
    DB, DS, _ = x_sample.shape
    NS = DB * DS
    T = SEQ + NS
    KT = D // P
    NCH = 3
    CH = T // NCH
    NB = SEQ // P
    PLE = p_prompt.shape[3]
    KP = PLE // P
    HD = cache_k.shape[4]
    H = sinks.shape[1]
    G = H // 2
    WB = cache_k.shape[2]
    CW = conv_w.shape[2]
    SCALE = float(HD) ** -0.5
    AW = H * HD
    LASTB = T - P
    assert T == NCH * CH and CH <= 512 and KT == 8 and HD == 64 and WB == P and G == 4 and CW == 4 * P

    C_Q, C_K, C_V = 0, AW, AW + P
    C_GA = AW + 2 * P
    C_BG, C_CG, C_HC, C_GC = (C_GA + AW + i * CW for i in range(4))

    A_TILES = [("v", 0, C_V), ("k", 0, C_K)] + [("q", t, C_Q) for t in range(4)]
    for j in range(4):
        A_TILES += [("cg", j, C_CG), ("hc", j, C_HC), ("gc", j, C_GC), ("bg", j, C_BG)]
    A_TILES += [("ga", t, C_GA) for t in range(4)]
    NA = len(A_TILES)
    A_SLOTS, B_SLOTS = NCH * NA, NCH * KT
    GROUPS = A_SLOTS + B_SLOTS + 2 * B_SLOTS
    FT = NA + 2 * KT

    V_TURN, KC_TURN, SC_TURN, QPACK = 3, 6, 7, 21
    AT0 = 24
    D0 = AT0 + 4 * NB + 2
    TAILS = 67

    def units_at(slot):
        out = []
        for u in range(2 * NB):
            at = AT0 + 2 * u
            out += [("pv", u)] * (slot == at + 3) + [("turn", u)] * (slot == at + 2)
            out += [("norm", u)] * (slot == at + 1) + [("scores", u)] * (slot == at)
        for g in range(2):
            at, u = D0 + 4 * g, 2 * NB + g
            out += [("pv", u)] * (slot == at + 4) + [("turn", u)] * (slot == at + 3) + [("norm", u)] * (slot == at + 2)
            out += [("dscores", u)] * (slot == at + 1) + [("dcache", u)] * (slot == at)
        order = ["pv", "turn", "norm", "dscores", "scores", "dcache"]
        return sorted(out, key=lambda x: order.index(x[0]))

    def loads_of(w):
        f = w % FT
        if f < NA:
            return 2 if A_TILES[f][0] in ("q", "ga") else 1
        return 3 if f < NA + KT else 2

    def loaded_count(w):
        return 16 * sum(loads_of(i) for i in range(w % 2, w + 1, 2))

    def last_group(w):
        l, f = divmod(w, FT)
        if f < NA + KT:
            return l * GROUPS + NCH * f + NCH - 1
        return l * GROUPS + A_SLOTS + B_SLOTS + 2 * (NCH * (f - NA - KT) + NCH) - 1

    def uses(bank, g):
        return (g + 3 - bank) // 4

    def gates(l, kind, j, c):
        return l * B_SLOTS + (0 if kind == "gc" else 4 * NCH) + NCH * j + c + 1

    def exps(l, u):
        return l * (10 * NB + 4) + (5 * (u + 1) if u < 2 * NB else 10 * NB + 2 * (u + 1 - 2 * NB))

    NSQ = B_SLOTS - NCH
    NTAIL = 5 + 2 * DS
    CONSTS = 16 * (2 + DEPTH * 4)

    with ExitStack() as ctx:
        at = [nc.sbuf_base + (-nc.sbuf_base) % 32]

        def place(name, shape, dtype, offset=None):
            n = 4
            for s in shape[1:]:
                n *= s
            if offset is None:
                offset = at[0]
                at[0] += n + (-n) % 32
            return nc.alloc_sbuf_tensor_at(name, shape, dtype, offset=offset), offset

        act, raw, rot, side, kcT, vc = [], [], [], [], [], []
        for i in range(2):
            a, off = place(f"act{i}", [P, 2, KT, T], F32R)
            lo = off + KT * T * 4
            act.append(a)
            raw.append(place(f"raw{i}", [P, 4, T], F32, off)[0])
            rot.append(place(f"rot{i}", [P, T], F32, lo)[0])
            side.append(place(f"side{i}", [P, DB, P], F32, lo + 4 * T)[0])
            kcT.append(place(f"kcT{i}", [P, DB, P], F32, lo + 4 * T + 4096)[0])
            vc.append(place(f"vc{i}", [P, DB, P], F32, lo + 4 * T + 8192)[0])
            if i == 0:
                xfin, _ = place("xfin", [P, KT, T], F32, off)
            else:
                xnat, _ = place("xnat", [P, NB + 1, D], F32, off)
        stage, _ = place("stage", [P, 2, KT + KP, P], F32)
        ws, _ = place("ws", [P, 2, 2, KT + KP, P], F32R)
        kT, off = place("kT", [P, T], F32)
        vnat, _ = place("vnat", [P, NB + 1, P], F32)
        cosT, _ = place("cosT", [P, T], F32)
        sinT, _ = place("sinT", [P, T], F32)
        pT, _ = place("pT", [P, 2, KP, T], F32R, off)
        rb, _ = place("rb", [P, T], F32)
        up, off = place("up", [P, 2 + SEQ], F32)
        us, _ = place("us", [P, DB, 2 + DS], F32)
        acc, _ = place("acc", [P, T], F32, off)
        yc, off = place("yc", [P, (NB + 1) * P], F32)
        diag, _ = place("diag", [P, NB + 1, P], F32, off)
        tmp, _ = place("tmp", [P, 2, CH], F32)
        gate, _ = place("gate", [P, 2, CH], F32)
        comb, _ = place("comb", [P, 4, P], F32)
        ptcp, _ = place("ptcp", [P, 2, 4 * P], F32)
        prev_mask, _ = place("prev_mask", [P, P], F32)
        cur_maskT, _ = place("cur_maskT", [P, P], F32)
        ident, _ = place("ident", [P, P], F32)
        ones, _ = place("ones", [P, P], F32)
        dmask, _ = place("dmask", [P, P + NS + G], F32)
        qp, _ = place("qp", [P, DB, G, DS], F32)
        scT, _ = place("scT", [P, 4, 2 * DB], F32)
        utail, _ = place("utail", [P, 4, 2 + NS], F32)
        gT, _ = place("gT", [P, DEPTH, KT], F32)
        cwT, _ = place("cwT", [P, DEPTH, 3, 4], F32)
        sink, _ = place("sink", [P, DEPTH, H], F32)
        sinkd, _ = place("sinkd", [P, DEPTH, 2], F32)
        nsink, _ = place("nsink", [P, DEPTH, H + 2], F32)
        st, _ = place("st", [P, 8, 4], F32)
        nr, _ = place("nr", [P, 6, NB + 1], F32)
        neg, _ = place("neg", [P, 1], F32)
        skt = ptcp[:, 1, 0:P]
        ytmp = yc[:, 0:T].rearrange("p (c n) -> p c n", c=NCH)
        pn = ptcp[:].rearrange("p a n -> p (a n)").rearrange("p (b n) -> p b n", b=4)
        gfb = ptcp[:].rearrange("p a n -> p (a n)")

        def psum(name, shape):
            return ctx.enter_context(nc.psum_tensor(name, shape, F32))

        ring = psum("ring", [P, 4, 512])
        pS = psum("pS", [P, 1024])
        pT1 = psum("pT1", [P, 512])
        pO = psum("pO", [P, 512])
        pS4 = pS[:].rearrange("p (h n) -> p h n", h=4)

        names = """const_made consts_in x_turned x_hi x_sq x_lo x_acc
            loaded0 loaded1 w_scaled w_hi w_lo w_used group_done free0 free1 free2 free3
            ss_done mean_done root_done r_done diag_done bcast_done rb_done
            rot_in roped tables_in v_turned v_taken kc_in kc_turned kc_taken sc_in sc_turned sc_taken
            vc_in q_packed cur_taken scores_done scores_taken negm_done exp_done probs_ready
            p_turned pt_taken pv_done o_taken dcache_done dcache_taken
            gate_out sum_ready hi_out mix_split mid_split out_split sig_out sq_out acc_done
            tail_ready tail_turned tail_taken tail_out p_in p_turned2 p_hi p_lo pad_ready
            gf_in y_turned y_ready y_out cache_out dve_step pool_step""".split()
        S = {n: ctx.enter_context(nc.semaphore(n)) for n in names}
        const_made, consts_in = S["const_made"], S["consts_in"]
        loaded = [S["loaded0"], S["loaded1"]]
        free = [S[f"free{i}"] for i in range(4)]
        x_in = [ctx.enter_context(nc.semaphore(f"x_in{b}")) for b in range(NB + 1)]
        group_done, w_hi, w_lo, w_used, w_scaled = (S[n] for n in ("group_done", "w_hi", "w_lo", "w_used", "w_scaled"))

        def cols(c):
            return slice(c * CH, (c + 1) * CH)

        def xblock(b):
            return (b * P, P) if b < NB else (SEQ, NS)

        block = ctx.enter_context(nc.Block())

        @block.sync
        def _(sp):
            for b in range(NB):
                sp.dma_start(xnat[:, b, :], x_prompt[0, b * P:(b + 1) * P, :]).then_inc(x_in[b], 16)
            sp.dma_start(xnat[0:NS, NB, :], x_sample.rearrange("b s d -> (b s) d")).then_inc(x_in[NB], 16)
            for l in range(DEPTH):
                for f in range(FT):
                    w = l * FT + f
                    s = w % 2
                    if w >= 2:
                        sp.wait_ge(w_lo, w - 1)
                        sp.wait_ge(w_hi, w - 1)
                    if f < NA:
                        kind, j, c0 = A_TILES[f]
                        src = w_in[l].rearrange("(k p) n -> p k n", p=P)
                        if kind in ("q", "ga"):
                            for i in range(2):
                                c = c0 + (j + 4 * i) * HD
                                sp.dma_start(stage[:, s, 0:KT, i * HD:(i + 1) * HD],
                                             src[:, :, c:c + HD]).then_inc(loaded[s], 16)
                        else:
                            c = c0 + j * P
                            sp.dma_start(stage[:, s, 0:KT, :], src[:, :, c:c + P]).then_inc(loaded[s], 16)
                    elif f < NA + KT:
                        c = (f - NA) * P
                        for i in range(2):
                            sp.dma_start(stage[i * HD:(i + 1) * HD, s, 0:4, :],
                                         w_out[l, i * 4 * HD:(i + 1) * 4 * HD, c:c + P]
                                         .rearrange("(t p) n -> p t n", p=HD)).then_inc(loaded[s], 16)
                        sp.dma_start(stage[:, s, 4:8, :], w_out[l, AW:D, c:c + P]
                                     .rearrange("(t p) n -> p t n", p=P)).then_inc(loaded[s], 16)
                    else:
                        c = (f - NA - KT) * P
                        sp.dma_start(stage[:, s, 0:KT, :], w_pg[l, :, c:c + P]
                                     .rearrange("(t p) n -> p t n", p=P)).then_inc(loaded[s], 16)
                        sp.dma_start(stage[:, s, KT:KT + KP, :], w_pp[l, :, c:c + P]
                                     .rearrange("(t p) n -> p t n", p=P)).then_inc(loaded[s], 16)
                    if f == 1:
                        if l == 0:
                            sp.wait_ge(S["x_turned"], NB + 1)
                        else:
                            sp.wait_ge(group_done, l * GROUPS)
                            sp.wait_ge(S["tail_out"], 16 * NTAIL * l)
                        mx = 1 - l % 2
                        sp.dma_start(cosT[:], rope_cos).then_inc(S["tables_in"], 16)
                        sp.dma_start(sinT[:], rope_sin).then_inc(S["tables_in"], 16)
                        sp.dma_start(comb[0:2 * DB, :, :].rearrange("p a n -> p (a n)"),
                                     state_conv[l].rearrange("b r n -> (b r) n")).then_inc(S["sc_in"], 16)
                        sp.dma_start(side[mx][:], cache_k[l].rearrange("b k g d -> k b (g d)")).then_inc(S["kc_in"], 16)
                        sp.dma_start(vc[mx][:], cache_v[l].rearrange("b k g d -> k b (g d)")).then_inc(S["vc_in"], 16)
                        for new, old in ((new_k_sample, cache_k), (new_v_sample, cache_v)):
                            sp.dma_start(new[l, :, 0:WB - DS].rearrange("b k g d -> b (k g d)"),
                                         old[l, :, DS:WB].rearrange("b k g d -> b (k g d)")).then_inc(S["cache_out"], 16)
                    if NA + 1 <= f < NA + 4:
                        i = f - NA - 1
                        if i == 0:
                            sp.wait_ge(S["tail_out"], 16 * NTAIL * (l + 1))
                            sp.wait_ge(S["pt_taken"], 2 * (2 * NB + 2) * (l + 1))
                            sp.wait_ge(S["pv_done"], (2 * NB + 2) * (l + 1))
                        else:
                            sp.wait_ge(S["p_turned2"], 3 * l + i)
                        if i < 2:
                            sp.dma_start(pn[:], p_prompt[l, 0, i * 4 * P:(i + 1) * 4 * P, :]
                                         .rearrange("(b p) n -> p b n", p=P)).then_inc(S["p_in"], 16)
                        else:
                            sp.dma_start(pn[0:NS, 0, :], p_sample[l].rearrange("b s n -> (b s) n"))\
                              .then_inc(S["p_in"], 16)
            sp.wait_ge(S["p_turned2"], 3 * DEPTH)
            sp.dma_start(gfb, g_final.rearrange("(a n) -> a n", a=1).to_broadcast([P, D])).then_inc(S["gf_in"], 16)
            for b in range(NB + 1):
                sp.wait_ge(S["y_ready"], b + 1)
                if b < NB:
                    sp.dma_start(y_prompt[0, b * P:(b + 1) * P, :], xnat[:, b, :]).then_inc(S["y_out"], 16)
                else:
                    sp.dma_start(y_sample.rearrange("b s d -> (b s) d"), xnat[P - NS:P, b, :]).then_inc(S["y_out"], 16)
            sp.wait_ge(S["y_out"], 16 * (NB + 1))
            sp.wait_ge(S["cache_out"], 16 * 2 * DEPTH)
            sp.wait_ge(S["tail_out"], 16 * NTAIL * DEPTH)

        @block.gpsimd
        def _(pool):
            with nc.allow_non_contiguous_dma("small"):
                pool.dma_start(gT[:], g_norm.rearrange("l (k p) -> p l k", p=P)).then_inc(consts_in, 16)
                for l in range(DEPTH):
                    for i in range(3):
                        pool.dma_start(cwT[:, l, i, :], conv_w[l, i].rearrange("(k p) -> p k", p=P))\
                            .then_inc(consts_in, 16)
                    pool.dma_start(sink[:, l, :], sinks[l:l + 1, :].to_broadcast([P, H])).then_inc(consts_in, 16)
                pool.dma_start(dmask[:], decode_mask).then_inc(consts_in, 16)
            pool.memset(ident[:], 0.0).then_inc(S["pool_step"], 1)
            pool.memset(prev_mask[:], 1.0).then_inc(S["pool_step"], 1)
            pool.memset(cur_maskT[:], 1.0).then_inc(S["pool_step"], 1)
            pool.wait_ge(S["pool_step"], 3)
            pool.affine_select(out=ident[:], in_=ident[:], compare_op=ALU.not_equal, fill=1.0, base=0,
                               pattern=[[-1, P]], channel_multiplier=1).then_inc(const_made, 1)
            pool.affine_select(out=prev_mask[:], in_=prev_mask[:], compare_op=ALU.is_gt, fill=0.0, base=0,
                               pattern=[[1, P]], channel_multiplier=-1).then_inc(const_made, 1)
            pool.affine_select(out=cur_maskT[:], in_=cur_maskT[:], compare_op=ALU.is_ge, fill=0.0, base=0,
                               pattern=[[1, P]], channel_multiplier=-1).then_inc(const_made, 1)
            pool.memset(ones[:], 1.0).then_inc(const_made, 1)
            pool.memset(neg[:], NEG).then_inc(const_made, 1)
            pool.wait_ge(consts_in, CONSTS)
            for l in range(DEPTH):
                for f in range(FT):
                    w = l * FT + f
                    s = w % 2
                    n = KT if f < NA + KT else KT + KP
                    pool.wait_ge(loaded[s], loaded_count(w))
                    if f < NA:
                        nc.gpsimd.tensor_tensor(stage[:, s, 0:n, :], stage[:, s, 0:n, :],
                                                gT[:, l, :].rearrange("p (k a) -> p k a", a=1).to_broadcast([P, n, P]),
                                                ALU.mult).then_inc(w_scaled, 1)
                    pool.wait_ge(w_hi, w + 1)
                    nc.gpsimd.tensor_tensor(ws[:, s, 1, 0:n, :], stage[:, s, 0:n, :],
                                            ws[:, s, 0, 0:n, :].bitcast(F32), ALU.subtract).then_inc(w_lo, 1)

        @block.tensor
        def _(pe):
            def group(g, w, x, tiles, cs, waits=None, last=None):
                out = ring[:, g % 4, 0:CH]
                if g >= 4:
                    pe.wait_ge(free[g % 4], g // 4)
                n = len(tiles)
                for i, (kw, kx) in enumerate(tiles):
                    if waits:
                        pe.wait_ge(*waits(i))
                    for wp, xp in ((0, 0), (0, 1), (1, 0)):
                        mm = nc.tensor.matmul(out, ws[:, w % 2, wp, kw, :], x[:, xp, kx, cs],
                                              start=(i == 0 and wp == 0 and xp == 0), stop=(i == n - 1 and wp == 1))
                mm.then_inc(group_done, 1)

            def attention(l, step, u):
                b, g = u // 2, u % 2
                mx = 1 - l % 2
                U = l * (2 * NB + 2) + u
                rows = slice(g * HD, (g + 1) * HD)
                q = raw[mx]
                if step == "scores":
                    if u == 0:
                        pe.wait_ge(S["roped"], 5 * (l + 1))
                        pe.wait_ge(S["kc_taken"], l + 1)
                        pe.wait_ge(S["sc_taken"], l + 1)
                    else:
                        pe.wait_ge(S["scores_taken"], U)
                    for t in range(4):
                        if b == 0:
                            mm = nc.tensor.matmul(pS4[:, t, P:2 * P], q[rows, t, 0:P], kT[rows, 0:P], start=True, stop=True)
                        else:
                            mm = nc.tensor.matmul(pS4[:, t, :], q[rows, t, b * P:(b + 1) * P],
                                                  kT[rows, (b - 1) * P:(b + 1) * P], start=True, stop=True)
                    mm.then_inc(S["scores_done"], 1)
                elif step == "dcache":
                    pe.wait_ge(S["q_packed"], l + 1)
                    pe.wait_ge(S["scores_taken"], U)
                    for i in range(DB):
                        mm = nc.tensor.matmul(pS[:, i * G * DS:(i + 1) * G * DS], kcT[mx][rows, i, :],
                                              qp[rows, i, :, :].rearrange("p a b -> p (a b)"), start=True, stop=True)
                    mm.then_inc(S["dcache_done"], 1)
                elif step == "dscores":
                    pe.wait_ge(S["dcache_taken"], 2 * l + g + 1)
                    nc.tensor.transpose(pS[:, 512:512 + P], skt, ident[:])
                    mm = nc.tensor.matmul(pS[:, 512 + P:512 + P + NS], qp[rows].rearrange("p a b c -> p (a b c)"),
                                          kT[rows, SEQ:T], start=True, stop=True)
                    mm.then_inc(S["scores_done"], 1)
                elif step == "turn":
                    pe.wait_ge(S["probs_ready"], U + 1)
                    if b < NB:
                        for t in range(4):
                            mm = nc.tensor.transpose(pT1[:, t * P:(t + 1) * P], comb[:, t, :], ident[:])
                    else:
                        flat = comb[:].rearrange("p a n -> p (a n)")
                        nc.tensor.transpose(pT1[:, 0:P], flat[:, 0:P], ident[:])
                        mm = nc.tensor.transpose(pT1[0:NS, P:2 * P], flat[:, P:P + NS], ident[:])
                    mm.then_inc(S["p_turned"], 1)
                elif step == "pv":
                    pe.wait_ge(S["pt_taken"], 2 * (U + 1))
                    if g == 0 and b > 0:
                        pe.wait_ge(S["o_taken"], l * (NB + 1) + b)
                    if b < NB:
                        mm = nc.tensor.matmul(pO[rows, :], vnat[:, b, rows], ptcp[:, 0, :], start=True, stop=(b == 0))
                        if b:
                            mm = nc.tensor.matmul(pO[rows, :], vnat[:, b - 1, rows], ptcp[:, 1, :], start=False, stop=True)
                    else:
                        pe.wait_ge(S["vc_in"], 16 * (l + 1))
                        nc.tensor.matmul(pO[rows, 0:P], vnat[0:NS, NB, rows], ptcp[0:NS, 1, 0:P], start=True, stop=False,
                                         skip_group_check=True)
                        for i in range(DB):
                            r = slice(i * G * DS, (i + 1) * G * DS)
                            mm = nc.tensor.matmul(pO[rows, r], vc[mx][:, i, rows], ptcp[:, 0, r], start=False,
                                                  stop=(i == DB - 1), skip_group_check=True)
                    mm.then_inc(S["pv_done"], 1)

            def norm_sums(n, acc_ready):
                pe.wait_ge(*acc_ready)
                for b in range(NB + 1):
                    t0 = b * P if b < NB else LASTB
                    mm = nc.tensor.matmul(pT1[:, b:b + 1], acc[:, t0:t0 + P], ones[:, 0:1], start=True, stop=True)
                mm.then_inc(S["ss_done"], 1)

            def broadcast(l):
                pe.wait_ge(S["diag_done"], l + 1)
                for b in range(NB):
                    nc.tensor.matmul(pS[:, b * P:(b + 1) * P], ones[:], diag[:, b, :], start=True, stop=True)
                mm = nc.tensor.matmul(pO[:, 0:P], ones[:], diag[:, NB, :], start=True, stop=True)
                mm.then_inc(S["bcast_done"], 1)

            pe.wait_ge(const_made, 5)
            for b in range(NB + 1):
                n = xblock(b)[1]
                pe.wait_ge(x_in[b], 16)
                if b >= 2:
                    pe.wait_ge(S["x_hi"], b - 1)
                    pe.wait_ge(S["x_sq"], b - 1)
                    pe.wait_ge(S["x_lo"], b - 1)
                for k in range(KT):
                    mm = nc.tensor.transpose(ring[:, 2 * (b % 2) + k // 4, (k % 4) * P:(k % 4) * P + n],
                                             xnat[0:n, b, k * P:(k + 1) * P], ident[0:n, 0:n])
                mm.then_inc(S["x_turned"], 1)
            pe.wait_ge(S["x_hi"], NB + 1)
            pe.wait_ge(S["x_sq"], NB + 1)
            pe.wait_ge(S["x_lo"], NB + 1)

            for l in range(DEPTH):
                xa, mx = act[l % 2], act[1 - l % 2]
                m = 1 - l % 2
                g0 = l * GROUPS
                for f in range(NA):
                    w = l * FT + f
                    pe.wait_ge(w_lo, w + 1)
                    for c in range(NCH):
                        s = NCH * f + c
                        waits = None
                        if l and f == 0:
                            waits = lambda i, c=c: (S["out_split"], (l - 1) * B_SLOTS + NCH * i + c + 1)
                        group(g0 + s, w, xa, [(k, k) for k in range(KT)], cols(c), waits)
                        if s == 0:
                            norm_sums(l, (S["x_acc"], NB + 1) if l == 0 else (S["acc_done"], l * NSQ))
                        if s == 1:
                            broadcast(l)
                        if s == V_TURN:
                            for g in range(g0, g0 + NCH):
                                pe.wait_ge(free[g % 4], uses(g % 4, g + 1))
                            pe.wait_ge(S["rb_done"], 2 * (l + 1))
                            for b in range(NB):
                                nc.tensor.transpose(pS[:, b * P:(b + 1) * P], rot[m][:, b * P:(b + 1) * P], ident[:])
                            mm = nc.tensor.transpose(pO[0:NS, 0:P], rot[m][:, SEQ:T], ident[:])
                            mm.then_inc(S["v_turned"], 1)
                        if s == KC_TURN:
                            pe.wait_ge(S["kc_in"], 16 * (l + 1))
                            pe.wait_ge(S["v_taken"], 2 * (l + 1))
                            for b in range(DB):
                                mm = nc.tensor.transpose(pS[:, b * P:(b + 1) * P], side[m][:, b, :], ident[:])
                            mm.then_inc(S["kc_turned"], 1)
                        if s == SC_TURN:
                            pe.wait_ge(S["sc_in"], 16 * (l + 1))
                            for j in range(4):
                                mm = nc.tensor.transpose(pO[:, j * 2 * DB:(j + 1) * 2 * DB], comb[0:2 * DB, j, :],
                                                         ident[0:2 * DB, 0:2 * DB])
                            mm.then_inc(S["sc_turned"], 1)
                        for step, u in units_at(s):
                            attention(l, step, u)
                        if s == TAILS:
                            pe.wait_ge(S["tail_ready"], 4 * (l + 1))
                            pe.wait_ge(S["scores_taken"], (2 * NB + 2) * (l + 1))
                            for j in range(4):
                                nc.tensor.transpose(pS[0:2 + NS, j * P:(j + 1) * P], utail[:, j, :], ident[:])
                            nc.tensor.transpose(pS[:, 512:512 + P], kT[:, SEQ - P:SEQ], ident[:])
                            mm = nc.tensor.transpose(pS[0:NS, 640:640 + P], kT[:, SEQ:T], ident[:])
                            mm.then_inc(S["tail_turned"], 1)
                g0 += A_SLOTS
                for f in range(KT):
                    w = l * FT + NA + f
                    pe.wait_ge(w_lo, w + 1)
                    for c in range(NCH):
                        waits = None
                        if f == 0:
                            waits = lambda i, c=c: (S["mix_split"], l * B_SLOTS + NCH * i + c + 1)
                        group(g0 + NCH * f + c, w, mx, [(k, k) for k in (4, 5, 6, 7, 0, 1, 2, 3)], cols(c), waits)
                        if c == 0 and 2 <= f < 5:
                            i = f - 2
                            pe.wait_ge(S["p_in"], 16 * (3 * l + i + 1))
                            if i == 0:
                                pe.wait_ge(S["tail_taken"], 3 * (l + 1))
                            else:
                                pe.wait_ge(S["p_hi"], 3 * l + i)
                                pe.wait_ge(S["p_lo"], 3 * l + i)
                            for k in range(KP):
                                for b in range(4 if i < 2 else 1):
                                    n = P if i < 2 else NS
                                    mm = nc.tensor.transpose(pS[:, k * 512 + b * P:k * 512 + b * P + n],
                                                             pn[0:n, b, k * P:(k + 1) * P], ident[0:n, 0:n])
                            mm.then_inc(S["p_turned2"], 1)
                g0 += B_SLOTS
                for f in range(KT):
                    w = l * FT + NA + KT + f
                    pe.wait_ge(w_lo, w + 1)
                    for c in range(NCH):
                        s = NCH * f + c
                        if s == 0:
                            pe.wait_ge(S["p_hi"], 3 * (l + 1))
                            pe.wait_ge(S["p_lo"], 3 * (l + 1))
                        group(g0 + 2 * s, w, pT, [(KT + k, k) for k in range(KP)], cols(c))
                        waits = None
                        if f == 0:
                            waits = lambda i, c=c: (S["mid_split"], l * B_SLOTS + NCH * i + c + 1)
                        group(g0 + 2 * s + 1, w, xa, [(k, k) for k in range(KT)], cols(c), waits)
            norm_sums(DEPTH, (S["acc_done"], DEPTH * NSQ))
            pe.wait_ge(S["out_split"], DEPTH * B_SLOTS)
            for i in range(4):
                pe.wait_ge(free[i], uses(i, DEPTH * GROUPS))
            for b in range(NB + 1):
                t0 = b * P if b < NB else LASTB
                if b >= 2:
                    pe.wait_ge(S["y_ready"], b - 1)
                for k in range(KT):
                    mm = nc.tensor.transpose(ring[:, 2 * (b % 2) + k // 4, (k % 4) * P:(k % 4 + 1) * P],
                                             xfin[:, k, t0:t0 + P], ident[:])
                mm.then_inc(S["y_turned"], 1)

        @block.scalar
        def _(sc):
            def split_weights(w):
                f = w % FT
                n = KT if f < NA + KT else KT + KP
                if f < NA:
                    sc.wait_ge(w_scaled, (w // FT) * NA + f + 1)
                else:
                    sc.wait_ge(loaded[w % 2], loaded_count(w))
                if w >= 2:
                    sc.wait_ge(group_done, last_group(w - 2) + 1)
                    sc.wait_ge(w_lo, w - 1)
                nc.scalar.activation(ws[:, w % 2, 0, 0:n, :], stage[:, w % 2, 0:n, :], ACT.Copy).then_inc(w_hi, 1)

            def bank(g):
                sc.wait_ge(group_done, g + 1)
                return ring[:, g % 4, 0:CH]

            def high(dst, s, ready):
                sc.wait_ge(*ready)
                nc.scalar.activation(dst, tmp[:, s % 2, :], ACT.Copy).then_inc(S["hi_out"], 1)

            split_weights(0)
            split_weights(1)
            for b in range(NB + 1):
                t0, n = xblock(b)
                sc.wait_ge(S["x_turned"], b + 1)
                src = ring[:, 2 * (b % 2):2 * (b % 2) + 2, :].rearrange("p a (k n) -> p (a k) n", n=P)[:, :, 0:n]
                nc.scalar.activation(act[0][:, 0, :, t0:t0 + n], src, ACT.Copy).then_inc(S["x_hi"], 1)
                if b:
                    sc.wait_ge(S["x_acc"], b)
                nc.scalar.activation(diag[:, 0:KT, 0:n], src, ACT.Square).then_inc(S["x_sq"], 1)

            sums = 0
            for l in range(DEPTH):
                xa, mx = act[l % 2], act[1 - l % 2]
                m = 1 - l % 2
                g0 = l * GROUPS
                for s in range(A_SLOTS):
                    f, c = s // NCH, s % NCH
                    w = l * FT + f
                    kind, j, _ = A_TILES[f]
                    g = g0 + s
                    freed = (free[g % 4], uses(g % 4, g + 1))
                    if c == 0 and w >= 1:
                        split_weights(w + 1)
                    if s and A_TILES[(s - 1) // NCH][0] == "ga":
                        sums += 1
                        high(mx[:, 0, A_TILES[(s - 1) // NCH][1], cols((s - 1) % NCH)], s, (S["sum_ready"], sums))
                    if s == 0:
                        sc.wait_ge(S["mean_done"], l + 1)
                        nc.scalar.activation(nr[:, 1, :], nr[:, 0, :], ACT.Sqrt).then_inc(S["root_done"], 1)
                    if s == 1:
                        sc.wait_ge(S["bcast_done"], l + 1)
                        nc.scalar.activation(rb[:, 0:SEQ], pS[:], ACT.Copy).then_inc(S["rb_done"], 1)
                        nc.scalar.activation(rb[:, SEQ:T], pO[:, P - NS:P], ACT.Copy).then_inc(S["rb_done"], 1)
                    if s == V_TURN:
                        sc.wait_ge(S["v_turned"], l + 1)
                        nc.scalar.activation(vnat[:, 0:NB, :], pS[:].rearrange("p (b n) -> p b n", n=P), ACT.Copy)\
                          .then_inc(S["v_taken"], 1)
                        nc.scalar.activation(vnat[0:NS, NB, :], pO[0:NS, 0:P], ACT.Copy).then_inc(S["v_taken"], 1)
                    if s == KC_TURN:
                        sc.wait_ge(S["kc_turned"], l + 1)
                        nc.scalar.activation(kcT[m][:], pS[:].rearrange("p (b n) -> p b n", n=P), ACT.Copy)\
                          .then_inc(S["kc_taken"], 1)
                    if s == SC_TURN:
                        sc.wait_ge(S["sc_turned"], l + 1)
                        nc.scalar.activation(scT[:], pO[:, 0:8 * DB].rearrange("p (j n) -> p j n", j=4), ACT.Copy)\
                          .then_inc(S["sc_taken"], 1)
                    if 1 <= f < 6 and c == NCH - 1:
                        i = f - 1
                        for h in range(g - NCH + 1, g + 1):
                            sc.wait_ge(free[h % 4], uses(h % 4, h + 1))
                        if i == 0:
                            sc.wait_ge(S["v_turned"], l + 1)
                        else:
                            sc.wait_ge(S["roped"], 5 * l + i)
                        src = kT[:] if i == 0 else raw[m][:, i - 1, :]
                        for a in range(4):
                            o = a ^ 1
                            sc.dma_start(rot[m][32 * a:32 * a + 32, :], src[32 * o:32 * o + 32, :])\
                              .then_inc(S["rot_in"], 16)
                    if kind in ("gc", "ga"):
                        sc.wait_ge(*freed)
                        nc.scalar.activation(gate[:, s % 2, :], gate[:, s % 2, :], ACT.Silu).then_inc(S["gate_out"], 1)
                    for step, u in units_at(s):
                        b, gg = u // 2, u % 2
                        U = l * (2 * NB + 2) + u
                        if step == "scores":
                            sc.wait_ge(S["scores_done"], U + 1)
                            nc.scalar.activation(comb[:], pS4[:, :, P:2 * P], ACT.Copy).then_inc(S["cur_taken"], 1)
                        elif step == "dcache":
                            sc.wait_ge(S["dcache_done"], 2 * l + gg + 1)
                            nc.scalar.activation(skt, pS[:, 0:P], ACT.Copy).then_inc(S["dcache_taken"], 1)
                        elif step == "norm":
                            sc.wait_ge(S["negm_done"], 2 * (U + 1))
                            if b < NB:
                                for t in range(4):
                                    nc.scalar.activation(comb[:, t, :], comb[:, t, :], ACT.Exp, bias=st[:, 1, t:t + 1],
                                                         scale=SCALE, accum_out=st[:, 4, t:t + 1]).then_inc(S["exp_done"], 1)
                                nc.scalar.activation(st[:, 3, :], st[:, 2, :], ACT.Exp).then_inc(S["exp_done"], 1)
                            else:
                                flat = comb[:].rearrange("p a n -> p (a n)")[:, 0:P + NS]
                                nc.scalar.activation(flat, flat, ACT.Exp, bias=st[:, 1, 0:1], scale=SCALE,
                                                     accum_out=st[:, 4, 0:1]).then_inc(S["exp_done"], 1)
                                nc.scalar.activation(st[:, 3, 0:1], st[:, 2, 0:1], ACT.Exp).then_inc(S["exp_done"], 1)
                        elif step == "pv" and gg == 1:
                            sc.wait_ge(S["pv_done"], U + 1)
                            if b < NB:
                                nc.scalar.activation(raw[m][:, :, b * P:(b + 1) * P],
                                                     pO[:].rearrange("p (t n) -> p t n", t=4), ACT.Copy)\
                                  .then_inc(S["o_taken"], 1)
                            else:
                                nc.scalar.activation(raw[m][:, :, SEQ:T].rearrange("p h (b s) -> p b h s", s=DS),
                                                     pO[:, 0:P].rearrange("p (b h s) -> p b h s", h=G, s=DS), ACT.Copy)\
                                  .then_inc(S["o_taken"], 1)
                    if kind == "bg":
                        high(mx[:, 0, 4 + j, cols(c)], s, freed)
                    if s == TAILS:
                        sc.wait_ge(S["tail_turned"], l + 1)
                        ctail = comb[:].rearrange("p a n -> p (a n)")[0:2 + NS, :]
                        nc.scalar.activation(ctail, pS[0:2 + NS, 0:512], ACT.Copy).then_inc(S["tail_taken"], 1)
                        nc.scalar.activation(ptcp[:, 0, 0:P], pS[:, 512:512 + P], ACT.Copy).then_inc(S["tail_taken"], 1)
                        nc.scalar.activation(ptcp[0:NS, 0, P:2 * P], pS[0:NS, 640:640 + P], ACT.Copy)\
                          .then_inc(S["tail_taken"], 1)
                        sc.wait_ge(S["tail_taken"], 3 * (l + 1))
                        out = S["tail_out"]
                        sc.dma_start(new_conv_prompt[l, 0], ctail[0:2, :]).then_inc(out, 16)
                        for r in range(2):
                            o = 2 + DS - 2 + r
                            sc.dma_start(new_conv_sample[l, :, r, :], ctail[o:o + DS * (DB - 1) + 1:DS, :]).then_inc(out, 16)
                        sc.dma_start(new_k_prompt[l, 0].rearrange("k g d -> k (g d)"), ptcp[:, 0, 0:P]).then_inc(out, 16)
                        sc.dma_start(new_v_prompt[l, 0].rearrange("k g d -> k (g d)"), vnat[:, NB - 1, :]).then_inc(out, 16)
                        for r in range(DS):
                            sc.dma_start(new_k_sample[l, :, WB - DS + r].rearrange("b g d -> b (g d)"),
                                         ptcp[r:r + DS * (DB - 1) + 1:DS, 0, P:2 * P]).then_inc(out, 16)
                            sc.dma_start(new_v_sample[l, :, WB - DS + r].rearrange("b g d -> b (g d)"),
                                         vnat[r:r + DS * (DB - 1) + 1:DS, NB, :]).then_inc(out, 16)
                sums += 1
                high(mx[:, 0, 3, cols(NCH - 1)], A_SLOTS, (S["sum_ready"], sums))
                g0 += A_SLOTS
                for s in range(B_SLOTS):
                    f, c = s // NCH, s % NCH
                    if c == 0:
                        split_weights(l * FT + NA + f + 1)
                    sums += 1
                    high(xa[:, 0, f, cols(c)], s, (S["sum_ready"], sums))
                    if c == 0 and 2 <= f < 5:
                        i = f - 2
                        sc.wait_ge(S["p_turned2"], 3 * l + i + 1)
                        t0, n = (i * 512, 512) if i < 2 else (SEQ, NS)
                        if i == 0:
                            sc.wait_ge(S["tail_out"], 16 * NTAIL * (l + 1))
                        nc.scalar.activation(pT[:, 0, :, t0:t0 + n], pS[:].rearrange("p (k n) -> p k n", k=KP)[:, :, 0:n],
                                             ACT.Copy).then_inc(S["p_hi"], 1)
                g0 += B_SLOTS
                for s in range(B_SLOTS):
                    f, c = s // NCH, s % NCH
                    w = l * FT + NA + KT + f
                    if c == 0 and w + 1 < DEPTH * FT:
                        split_weights(w + 1)
                    g = g0 + 2 * s + 1
                    src = bank(g)
                    if s >= 2:
                        sc.wait_ge(free[(g - 5) % 4], uses((g - 5) % 4, g - 4))
                    nc.scalar.activation(gate[:, s % 2, :], src, ACT.Sigmoid).then_inc(free[g % 4], 1)
                    if l < DEPTH - 1:
                        sums += 1
                        high(mx[:, 0, f, cols(c)], s, (S["sum_ready"], sums))
                        last = tmp[:, s % 2, :]
                    else:
                        sc.wait_ge(S["out_split"], l * B_SLOTS + s + 1)
                        last = xfin[:, f, cols(c)]
                    if s >= 2 * NCH:
                        sc.wait_ge(S["acc_done"], l * NSQ + s - 2 * NCH + 1)
                    nc.scalar.activation(acc[:, cols(c)] if f == 0 else ytmp[:, c, :], last, ACT.Square)\
                      .then_inc(S["sq_out"], 1)
            sc.wait_ge(S["mean_done"], DEPTH + 1)
            nc.scalar.activation(nr[:, 1, :], nr[:, 0, :], ACT.Sqrt).then_inc(S["root_done"], 1)

        @block.vector
        def _(ve):
            V = nc.vector
            steps = [0]

            def link(ins):
                steps[0] += 1
                ins.then_inc(S["dve_step"], 1)
                ve.wait_ge(S["dve_step"], steps[0])

            def norm_scale(n):
                ve.wait_ge(S["ss_done"], n + 1)
                V.tensor_scalar(nr[:, 0, :], pT1[:, 0:NB + 1], 1.0 / D, EPS, ALU.mult, ALU.add).then_inc(S["mean_done"], 1)
                ve.wait_ge(S["root_done"], n + 1)
                link(V.reciprocal(nr[:, 2, :], nr[:, 1, :]))
                link(V.tensor_tensor(nr[:, 3, :], nr[:, 2, :], nr[:, 2, :], ALU.mult))
                link(V.tensor_tensor(nr[:, 4, :], nr[:, 3, :], nr[:, 0, :], ALU.mult))
                link(V.tensor_scalar(nr[:, 3, :], nr[:, 4, :], -0.5, 1.5, ALU.mult, ALU.add))
                link(V.tensor_tensor(nr[:, 5, :], nr[:, 3, :], nr[:, 2, :], ALU.mult))

            def bank(g):
                ve.wait_ge(group_done, g + 1)
                return ring[:, g % 4, 0:CH]

            highs = [0]

            def low(x, t, c, s, done):
                dst, hi = x[:, 1, t, cols(c)], x[:, 0, t, cols(c)]
                highs[0] += 1
                ve.wait_ge(S["hi_out"], highs[0])
                V.tensor_tensor(dst, tmp[:, s % 2, :], hi.bitcast(F32), ALU.subtract).then_inc(done, 1)

            ve.wait_ge(consts_in, CONSTS)
            link(V.tensor_scalar(nsink[:, :, 0:H], sink[:], -1.0, None, ALU.mult))
            pick = st[:, 0:2 * DEPTH, :]
            link(V.tensor_tensor(pick, sink[:].rearrange("p l (g h) -> p (l g) h", h=G),
                                 dmask[:, P + NS:].rearrange("p (a h) -> p a h", a=1).to_broadcast([P, 2 * DEPTH, G]),
                                 ALU.mult))
            link(V.tensor_reduce(sinkd[:].rearrange("p l g -> p (l g)"), pick, AX.X, ALU.add))
            link(V.tensor_scalar(nsink[:, :, H:H + 2], sinkd[:], -1.0, None, ALU.mult))
            ve.wait_ge(const_made, 5)
            for b in range(NB + 1):
                t0, n = xblock(b)
                ve.wait_ge(S["x_hi"], b + 1)
                ve.wait_ge(S["x_sq"], b + 1)
                src = ring[:, 2 * (b % 2):2 * (b % 2) + 2, :].rearrange("p a (k n) -> p (a k) n", n=P)[:, :, 0:n]
                V.tensor_tensor(act[0][:, 1, :, t0:t0 + n], src, act[0][:, 0, :, t0:t0 + n].bitcast(F32),
                                ALU.subtract).then_inc(S["x_lo"], 1)
                V.tensor_reduce(acc[:, t0:t0 + n], diag[:, 0:KT, 0:n].rearrange("p k n -> p n k"), AX.X, ALU.add)\
                 .then_inc(S["x_acc"], 1)
            ve.wait_ge(S["x_acc"], NB + 1)

            def add_squares(l, s):
                f, c = s // NCH, s % NCH
                ve.wait_ge(S["sq_out"], l * B_SLOTS + s + 1)
                if f == 0:
                    return
                if f >= 2:
                    ve.wait_ge(S["acc_done"], l * NSQ + s - 2 * NCH + 1)
                V.tensor_tensor(acc[:, cols(c)], acc[:, cols(c)], ytmp[:, c, :], ALU.add).then_inc(S["acc_done"], 1)

            for l in range(DEPTH):
                xa, mx = act[l % 2], act[1 - l % 2]
                m = 1 - l % 2
                g0 = l * GROUPS
                norm_scale(l)
                V.tensor_tensor(diag[:], ident[:].rearrange("p (a n) -> p a n", a=1).to_broadcast([P, NB + 1, P]),
                                     nr[:, 5, :].rearrange("p (b a) -> p b a", a=1).to_broadcast([P, NB + 1, P]),
                                     ALU.mult).then_inc(S["diag_done"], 1)
                ve.wait_ge(S["rb_done"], 2 * (l + 1))
                link(V.memset(up[:, 0:2], 0.0))

                def behind(s):
                    if s >= 2 and A_TILES[(s - 2) // NCH][0] == "ga":
                        low(mx, A_TILES[(s - 2) // NCH][1], (s - 2) % NCH, s - 1, S["mix_split"])
                    if not s or s > A_SLOTS:
                        return
                    kind, j, _ = A_TILES[(s - 1) // NCH]
                    c = (s - 1) % NCH
                    gt = gate[:, (s - 1) % 2, :]
                    if kind == "bg":
                        low(mx, 4 + j, c, s - 1, S["mix_split"])
                    elif kind == "gc":
                        ve.wait_ge(S["gate_out"], gates(l, kind, j, c))
                        link(V.tensor_tensor(ytmp[:, c, :], ytmp[:, c, :], gt, ALU.mult))
                    elif kind == "ga":
                        ve.wait_ge(S["gate_out"], gates(l, kind, j, c))
                        ve.wait_ge(S["o_taken"], (l + 1) * (NB + 1))
                        V.tensor_tensor(tmp[:, s % 2, :], gt, raw[m][:, j, cols(c)], ALU.mult).then_inc(S["sum_ready"], 1)

                for s in range(A_SLOTS):
                    f, c = s // NCH, s % NCH
                    kind, j, _ = A_TILES[f]
                    behind(s)
                    g = g0 + s
                    src = bank(g)
                    r = rb[:, cols(c)]
                    fr = free[g % 4]
                    if kind in ("v", "k", "q"):
                        dst = {"v": rot[m][:, cols(c)], "k": kT[:, cols(c)], "q": raw[m][:, j, cols(c)]}[kind]
                        V.tensor_tensor(dst, src, r, ALU.mult).then_inc(fr, 1)
                    elif kind == "cg":
                        V.tensor_tensor(ytmp[:, c, :], src, r, ALU.mult).then_inc(fr, 1)
                    elif kind == "hc":
                        t = tmp[:, s % 2, :]
                        V.tensor_tensor(t, src, r, ALU.mult).then_inc(fr, 1)
                        ve.wait_ge(fr, uses(g % 4, g + 1))
                        ve.wait_ge(free[(g - NCH) % 4], uses((g - NCH) % 4, g - NCH + 1))
                        n = min(CH, SEQ - c * CH)
                        link(V.tensor_tensor(up[:, 2 + c * CH:2 + c * CH + n], t[:, 0:n], ytmp[:, c, 0:n], ALU.mult))
                        w3 = [cwT[:, l, i, j:j + 1] for i in range(3)]
                        link(V.tensor_scalar(ytmp[:, c, 0:n], up[:, c * CH:c * CH + n], w3[0], None, ALU.mult))
                        for i in (1, 2):
                            link(V.scalar_tensor_tensor(ytmp[:, c, 0:n], up[:, c * CH + i:c * CH + i + n], w3[i],
                                                        ytmp[:, c, 0:n], ALU.mult, ALU.add))
                        if c == NCH - 1:
                            if j == 0:
                                ve.wait_ge(S["sc_taken"], l + 1)
                            link(V.tensor_copy(us[:, :, 0:2], scT[:, j, :].rearrange("p (b r) -> p b r", r=2)))
                            link(V.tensor_tensor(us[:, :, 2:2 + DS], t[:, n:CH].rearrange("p (b s) -> p b s", s=DS),
                                                 ytmp[:, c, n:CH].rearrange("p (b s) -> p b s", s=DS), ALU.mult))
                            ys = ytmp[:, c, n:CH].rearrange("p (b s) -> p b s", s=DS)
                            link(V.tensor_scalar(ys, us[:, :, 0:DS], w3[0], None, ALU.mult))
                            for i in (1, 2):
                                link(V.scalar_tensor_tensor(ys, us[:, :, i:i + DS], w3[i], ys, ALU.mult, ALU.add))
                            link(V.tensor_copy(utail[:, j, 0:2], up[:, SEQ:SEQ + 2]))
                            V.tensor_copy(utail[:, j, 2:2 + NS].rearrange("p (b s) -> p b s", s=DS),
                                          us[:, :, 2:2 + DS]).then_inc(S["tail_ready"], 1)
                    elif kind == "gc":
                        gt = gate[:, s % 2, :]
                        link(V.tensor_tensor(ytmp[:, c, :], ytmp[:, c, :], r, ALU.mult))
                        V.tensor_tensor(gt, src, r, ALU.mult).then_inc(fr, 1)
                    elif kind == "bg":
                        V.tensor_tensor(tmp[:, s % 2, :], src, ytmp[:, c, :], ALU.mult).then_inc(fr, 1)
                    elif kind == "ga":
                        V.tensor_tensor(gate[:, s % 2, :], src, r, ALU.mult).then_inc(fr, 1)
                    if 2 <= f < 7 and c == 1:
                        i = f - 2
                        x = kT[:] if i == 0 else raw[m][:, i - 1, :]
                        ve.wait_ge(S["tables_in"], 32 * (l + 1))
                        ve.wait_ge(S["rot_in"], 64 * (5 * l + i + 1))
                        link(V.tensor_tensor(rot[m][:], rot[m][:], sinT[:], ALU.mult))
                        link(V.tensor_tensor(x, x, cosT[:], ALU.mult))
                        V.tensor_tensor(x, x, rot[m][:], ALU.add).then_inc(S["roped"], 1)
                    if s == QPACK:
                        ve.wait_ge(S["roped"], 5 * (l + 1))
                        V.tensor_copy(qp[:], raw[m][:, :, SEQ:T].rearrange("p h (b s) -> p b h s", s=DS))\
                         .then_inc(S["q_packed"], 1)
                    for step, u in units_at(s):
                        b, gg = u // 2, u % 2
                        U = l * (2 * NB + 2) + u
                        dec = b == NB
                        n = 1 if dec else 4
                        flat = comb[:].rearrange("p a n -> p (a n)")[:, 0:P + NS]
                        if step in ("scores", "dscores"):
                            if dec:
                                ve.wait_ge(S["scores_done"], U + 1)
                                V.tensor_tensor(flat, pS[:, 512:512 + P + NS], dmask[:, 0:P + NS], ALU.add).then_inc(S["scores_taken"], 1)
                                ve.wait_ge(S["scores_taken"], U + 1)
                                link(V.tensor_reduce(st[:, 0, 0:1], flat, AX.X, ALU.max))
                                sk, nsk = sinkd[:, l, gg:gg + 1], nsink[:, l, H + gg:H + gg + 1]
                            else:
                                ve.wait_ge(S["cur_taken"], l * 2 * NB + u + 1)
                                mask = prev_mask[:].bitcast(U32).rearrange("p (a n) -> p a n", a=1).to_broadcast([P, 4, P])
                                data = pS4[:, :, 0:P] if b else neg[:].rearrange("p (a n) -> p a n", a=1).to_broadcast([P, 4, P])
                                V.copy_predicated(comb[:], mask, data).then_inc(S["scores_taken"], 1)
                                ve.wait_ge(S["scores_taken"], U + 1)
                                link(V.tensor_reduce(st[:, 0, :], comb[:], AX.X, ALU.max))
                                sk, nsk = sink[:, l, gg * G:(gg + 1) * G], nsink[:, l, gg * G:(gg + 1) * G]
                            V.scalar_tensor_tensor(st[:, 1, 0:n], st[:, 0, 0:n], -SCALE, nsk, ALU.mult, ALU.min)\
                             .then_inc(S["negm_done"], 1)
                            ve.wait_ge(S["negm_done"], 2 * U + 1)
                            V.tensor_tensor(st[:, 2, 0:n], st[:, 1, 0:n], sk, ALU.add).then_inc(S["negm_done"], 1)
                        elif step == "norm":
                            ve.wait_ge(S["exp_done"], exps(l, u))
                            link(V.tensor_tensor(st[:, 5, 0:n], st[:, 4, 0:n], st[:, 3, 0:n], ALU.add))
                            link(V.reciprocal(st[:, 6, 0:n], st[:, 5, 0:n]))
                            if dec:
                                V.tensor_scalar(flat, flat, st[:, 6, 0:1], None, ALU.mult).then_inc(S["probs_ready"], 1)
                            else:
                                V.tensor_tensor(comb[:], comb[:], st[:, 6, :].rearrange("p (a n) -> p a n", n=1)
                                                .to_broadcast([P, 4, P]), ALU.mult).then_inc(S["probs_ready"], 1)
                        elif step == "turn":
                            ve.wait_ge(S["p_turned"], U + 1)
                            if dec:
                                V.tensor_copy(ptcp[:, 0, 0:P], pT1[:, 0:P]).then_inc(S["pt_taken"], 1)
                                V.tensor_copy(ptcp[0:NS, 1, 0:P], pT1[0:NS, P:2 * P]).then_inc(S["pt_taken"], 1)
                            else:
                                pt = pT1[:].rearrange("p (a n) -> p a n", a=4)
                                V.tensor_tensor(ptcp[:, 0, :].rearrange("p (a n) -> p a n", a=4), pt,
                                                cur_maskT[:].rearrange("p (a n) -> p a n", a=1).to_broadcast([P, 4, P]),
                                                ALU.mult).then_inc(S["pt_taken"], 1)
                                ve.wait_ge(S["pt_taken"], 2 * U + 1)
                                V.tensor_tensor(ptcp[:, 1, :], pT1[:], ptcp[:, 0, :], ALU.subtract)\
                                 .then_inc(S["pt_taken"], 1)
                behind(A_SLOTS)
                behind(A_SLOTS + 1)
                ve.wait_ge(S["mix_split"], (l + 1) * B_SLOTS)
                g0 += A_SLOTS
                for s in range(B_SLOTS):
                    f, c = s // NCH, s % NCH
                    if s:
                        low(xa, (s - 1) // NCH, (s - 1) % NCH, s - 1, S["mid_split"])
                    g = g0 + s
                    t = tmp[:, s % 2, :]
                    V.tensor_tensor(t, bank(g), xa[:, 0, f, cols(c)].bitcast(F32), ALU.add).then_inc(free[g % 4], 1)
                    ve.wait_ge(free[g % 4], uses(g % 4, g + 1))
                    V.tensor_tensor(t, t, xa[:, 1, f, cols(c)].bitcast(F32), ALU.add).then_inc(S["sum_ready"], 1)
                    if c == 0 and 2 <= f < 5:
                        i = f - 2
                        ve.wait_ge(S["p_hi"], 3 * l + i + 1)
                        t0, n = (i * 512, 512) if i < 2 else (SEQ, NS)
                        V.tensor_tensor(pT[:, 1, :, t0:t0 + n], pS[:].rearrange("p (k n) -> p k n", k=KP)[:, :, 0:n],
                                        pT[:, 0, :, t0:t0 + n].bitcast(F32), ALU.subtract).then_inc(S["p_lo"], 1)
                low(xa, KT - 1, NCH - 1, B_SLOTS - 1, S["mid_split"])
                g0 += B_SLOTS
                for s in range(B_SLOTS):
                    f, c = s // NCH, s % NCH
                    if s:
                        if l < DEPTH - 1:
                            low(mx, (s - 1) // NCH, (s - 1) % NCH, s - 1, S["out_split"])
                        add_squares(l, s - 1)
                    g = g0 + 2 * s
                    src = bank(g)
                    t = tmp[:, s % 2, :]
                    ve.wait_ge(free[(g + 1) % 4], uses((g + 1) % 4, g + 2))
                    V.tensor_tensor(t, src, gate[:, s % 2, :], ALU.mult).then_inc(free[g % 4], 1)
                    ve.wait_ge(free[g % 4], uses(g % 4, g + 1))
                    link(V.tensor_tensor(t, t, xa[:, 0, f, cols(c)].bitcast(F32), ALU.add))
                    if l < DEPTH - 1:
                        V.tensor_tensor(t, t, xa[:, 1, f, cols(c)].bitcast(F32), ALU.add).then_inc(S["sum_ready"], 1)
                    else:
                        V.tensor_tensor(xfin[:, f, cols(c)], t, xa[:, 1, f, cols(c)].bitcast(F32), ALU.add)\
                         .then_inc(S["out_split"], 1)
                if l < DEPTH - 1:
                    low(mx, KT - 1, NCH - 1, B_SLOTS - 1, S["out_split"])
                add_squares(l, B_SLOTS - 1)
            norm_scale(DEPTH)
            ve.wait_ge(S["gf_in"], 16)
            for b in range(NB + 1):
                ve.wait_ge(S["y_turned"], b + 1)
                V.scalar_tensor_tensor(xnat[:, b, :], ring[:, 2 * (b % 2):2 * (b % 2) + 2, :].rearrange("p a n -> p (a n)"),
                                       nr[:, 5, b:b + 1], gfb, ALU.mult, ALU.mult).then_inc(S["y_ready"], 1)


_INS = ["x_prompt", "x_sample", "cache_k", "cache_v", "state_conv", "p_prompt", "p_sample", "g_norm", "w_in",
        "sinks", "conv_w", "w_out", "w_pg", "w_pp", "g_final"]


def _constants(seq, batch, steps, past, head_dim, group, window):
    import numpy as np

    inv = (10000.0 ** (-np.arange(0, head_dim, 2) / head_dim)).astype(np.float32)
    pos = np.concatenate([np.arange(seq), np.tile(past + np.arange(steps), batch)]).astype(np.float32)
    ang = (inv[:, None] * pos[None, :]).astype(np.float64)
    cos, sin = np.cos(ang).astype(np.float32), np.sin(ang).astype(np.float32)
    b, h, s = (a.ravel()[:, None] for a in np.indices((batch, group, steps)))
    cached = np.arange(window)[None, :] > s
    kb, ks = (a.ravel()[None, :] for a in np.indices((batch, steps)))
    new = (kb == b) & (ks <= s)
    mask = np.where(np.concatenate([cached, new], 1), 0.0, -1e30)
    flags = np.arange(group)[None, :] == h
    return (np.tile(cos, (4, 1)), np.concatenate([-sin, sin] * 2, 0),
            np.concatenate([mask, flags], 1).astype(np.float32))


def kernel(**inputs):
    import numpy as _np
    import concourse.bacc as _bacc
    from concourse import mybir as _mybir
    from concourse.bass_utils import run_bass_kernel_spmd as _run

    nc = _bacc.Bacc("TRN2", target_bir_lowering=False, num_devices=1)
    arrays, args = {}, []

    def give(name, a):
        arrays[f"in_{name}_dram"] = a
        args.append(nc.dram_tensor(f"in_{name}_dram", a.shape, _mybir.dt.from_np(a.dtype), kind="ExternalInput").ap())

    for name in _INS:
        give(name, _np.ascontiguousarray(inputs[name]))
    shape = {n: inputs[n].shape for n in _INS}
    depth, batch, window, kv, head_dim = shape["cache_k"]
    tables = _constants(shape["x_prompt"][1], batch, shape["x_sample"][1], 4096, head_dim,
                        shape["sinks"][1] // kv, window)
    for name, a in zip(("rope_cos", "rope_sin", "decode_mask"), tables):
        give(name, _np.ascontiguousarray(a))
    f32 = _mybir.dt.float32
    conv = shape["state_conv"]
    outs = [shape["x_prompt"], shape["x_sample"], (depth, 1, window, kv, head_dim), (depth, 1, window, kv, head_dim),
            (depth, 1, conv[2], conv[3]), shape["cache_k"], shape["cache_v"], conv]
    for i, s in enumerate(outs):
        args.append(nc.dram_tensor(f"out_{i}_dram", s, f32, kind="ExternalOutput").ap())
    hybrid_trunk(nc, *args)
    r = _run(nc, [arrays], core_ids=[0])
    return tuple(r.results[0][f"out_{i}_dram"] for i in range(len(outs)))
```

```python
from contextlib import ExitStack

import concourse.bass as bass
from concourse import mybir

F32 = mybir.dt.float32
F32R = mybir.dt.float32r
U32 = mybir.dt.uint32
ALU = mybir.AluOpType
ACT = mybir.ActivationFunctionType
AX = mybir.AxisListType
P = 128
NEG = -1e30
EPS = 1e-6


def hybrid_trunk(nc, x_prompt, x_sample, cache_k, cache_v, state_conv, p_prompt, p_sample, g_norm, w_in,
                 sinks, conv_w, w_out, w_pg, w_pp, g_final, rope_cos, rope_sin, decode_mask,
                 y_prompt, y_sample, new_k_prompt, new_v_prompt, new_conv_prompt,
                 new_k_sample, new_v_sample, new_conv_sample):
    DEPTH, D = g_norm.shape
    SEQ = x_prompt.shape[1]
    DB, DS, _ = x_sample.shape
    NS = DB * DS
    T = SEQ + NS
    KT = D // P
    NCH = 3
    CH = T // NCH
    NB = SEQ // P
    PLE = p_prompt.shape[3]
    KP = PLE // P
    HD = cache_k.shape[4]
    H = sinks.shape[1]
    G = H // 2
    WB = cache_k.shape[2]
    CW = conv_w.shape[2]
    SCALE = float(HD) ** -0.5
    AW = H * HD
    LASTB = T - P
    assert T == NCH * CH and CH <= 512 and KT == 8 and HD == 64 and WB == P and G == 4 and CW == 4 * P

    C_Q, C_K, C_V = 0, AW, AW + P
    C_GA = AW + 2 * P
    C_BG, C_CG, C_HC, C_GC = (C_GA + AW + i * CW for i in range(4))

    A_TILES = [("v", 0, C_V), ("k", 0, C_K)] + [("q", t, C_Q) for t in range(4)]
    for j in range(4):
        A_TILES += [("cg", j, C_CG), ("hc", j, C_HC), ("gc", j, C_GC), ("bg", j, C_BG)]
    A_TILES += [("ga", t, C_GA) for t in range(4)]
    NA = len(A_TILES)
    A_SLOTS, B_SLOTS = NCH * NA, NCH * KT
    GROUPS = A_SLOTS + B_SLOTS + 2 * B_SLOTS
    FT = NA + 2 * KT

    BCAST, V_TURN, KC_TURN, SC_TURN, QPACK = (3, 2), 5, 7, 8, 21
    AT0 = 24
    D0 = AT0 + 4 * NB + 2
    TAILS = 67

    def units_at(slot):
        out = []
        for u in range(2 * NB):
            at = AT0 + 2 * u
            out += [("pv", u)] * (slot == at + 4) + [("turn", u)] * (slot == at + 2)
            out += [("norm", u)] * (slot == at + 1) + [("scores", u)] * (slot == at)
            out += [("split", u)] * (slot == at - 2)
        for g in range(2):
            at, u = D0 + 4 * g, 2 * NB + g
            out += [("pv", u)] * (slot == at + 4) + [("turn", u)] * (slot == at + 3) + [("norm", u)] * (slot == at + 2)
            out += [("dscores", u)] * (slot == at + 1) + [("dcache", u)] * (slot == at)
        order = ["pv", "turn", "split", "norm", "dscores", "scores", "dcache"]
        return sorted(out, key=lambda x: order.index(x[0]))

    def loads_of(w):
        f = w % FT
        if f < NA:
            return 2 if A_TILES[f][0] in ("q", "ga") else 1
        return 3 if f < NA + KT else 2

    def loaded_count(w):
        return 16 * sum(loads_of(i) for i in range(w % 2, w + 1, 2))

    def last_group(w):
        l, f = divmod(w, FT)
        if f < NA + KT:
            return l * GROUPS + NCH * f + NCH - 1
        return l * GROUPS + A_SLOTS + B_SLOTS + 2 * (NCH * (f - NA - KT) + NCH) - 1

    def uses(bank, g):
        return (g + 3 - bank) // 4

    def gates(l, kind, j, c):
        return l * B_SLOTS + (0 if kind == "gc" else 4 * NCH) + NCH * j + c + 1

    def exps(l, u):
        return l * (10 * NB + 4) + (5 * (u + 1) if u < 2 * NB else 10 * NB + 2 * (u + 1 - 2 * NB))

    NSQ = B_SLOTS - NCH
    NTAIL = 5 + 2 * DS
    CONSTS = 16 * (1 + DEPTH * 4)

    with ExitStack() as ctx:
        at = [nc.sbuf_base + (-nc.sbuf_base) % 32]

        def place(name, shape, dtype, offset=None):
            n = 4
            for s in shape[1:]:
                n *= s
            if offset is None:
                offset = at[0]
                at[0] += n + (-n) % 32
            return nc.alloc_sbuf_tensor_at(name, shape, dtype, offset=offset), offset

        act, raw, rot, qps, side, kcT, vc = [], [], [], [], [], [], []
        for i in range(2):
            a, off = place(f"act{i}", [P, 2, KT, T], F32R)
            lo = off + KT * T * 4
            act.append(a)
            raw.append(place(f"raw{i}", [P, 4, T], F32, off)[0])
            rot.append(place(f"rot{i}", [P, T], F32, lo)[0])
            qps.append(place(f"qp{i}", [P, DB, G, DS], F32, lo)[0])
            side.append(place(f"side{i}", [P, DB, P], F32, lo + 4 * T)[0])
            kcT.append(place(f"kcT{i}", [P, DB, P], F32, lo + 4 * T + 4096)[0])
            vc.append(place(f"vc{i}", [P, DB, P], F32, lo + 4 * T + 8192)[0])
            if i == 0:
                xfin, _ = place("xfin", [P, KT, T], F32, off)
            else:
                xnat, _ = place("xnat", [P, NB + 1, D], F32, off)
        stage, _ = place("stage", [P, 2, KT + KP, P], F32)
        ws, _ = place("ws", [P, 2, 2, KT + KP, P], F32R)
        kT, off = place("kT", [P, T], F32)
        vnat, _ = place("vnat", [P, NB + 1, P], F32)
        cosT, cos_at = place("cosT", [P, T], F32)
        sinT, _ = place("sinT", [P, T], F32)
        qst, _ = place("qst", [P, 2, G, P], F32R, cos_at)
        kst, _ = place("kst", [P, 2, 2, 2 * P], F32R, cos_at + 2 * G * P * 4)
        pT, _ = place("pT", [P, 2, KP, T], F32R, off)
        rb, _ = place("rb", [P, T], F32)
        up, off = place("up", [P, 2 + SEQ], F32)
        us, _ = place("us", [P, DB, 2 + DS], F32)
        acc, _ = place("acc", [P, T], F32, off)
        yc, off = place("yc", [P, (NB + 1) * P], F32)
        diag, _ = place("diag", [P, NB + 1, P], F32, off)
        tmp, _ = place("tmp", [P, 2, CH], F32)
        gate, _ = place("gate", [P, 2, CH], F32)
        comb, _ = place("comb", [P, 4, P], F32)
        ptcp, _ = place("ptcp", [P, 2, 4 * P], F32)
        prev_mask, _ = place("prev_mask", [P, P], F32)
        cur_maskT, _ = place("cur_maskT", [P, P], F32)
        ident, _ = place("ident", [P, P], F32)
        ones, _ = place("ones", [P, P], F32)
        dmask, _ = place("dmask", [P, P + NS + G], F32)
        scT, _ = place("scT", [P, 4, 2 * DB], F32)
        utail, _ = place("utail", [P, 4, 2 + NS], F32)
        gT, _ = place("gT", [P, DEPTH + 1, KT], F32)
        cwT, _ = place("cwT", [P, DEPTH, 3, 4], F32)
        sink, _ = place("sink", [P, DEPTH, H], F32)
        sinkd, _ = place("sinkd", [P, DEPTH, 2], F32)
        nsink, _ = place("nsink", [P, DEPTH, H + 2], F32)
        st, _ = place("st", [P, 8, 4], F32)
        nr, _ = place("nr", [P, 7, NB + 1], F32)
        neg, _ = place("neg", [P, 1], F32)
        skt = ptcp[:, 1, 0:P]
        ytmp = yc[:, 0:T].rearrange("p (c n) -> p c n", c=NCH)
        pn = ptcp[:].rearrange("p a n -> p (a n)").rearrange("p (b n) -> p b n", b=4)
        gfb = ptcp[:].rearrange("p a n -> p (a n)")

        def psum(name, shape):
            return ctx.enter_context(nc.psum_tensor(name, shape, F32))

        ring = psum("ring", [P, 4, 512])
        aux = psum("aux", [P, 4, 512])
        pS = aux[:, 0:2, :].rearrange("p a n -> p (a n)")
        pT1 = aux[:, 2, :]
        pO = aux[:, 3, :]
        pS4 = pS.rearrange("p (h n) -> p h n", h=4)

        names = """const_made g_in consts_in x_turned x_hi x_sq x_lo
            loaded0 loaded1 w_scaled w_hi w_lo w_used group_done free0 free1 free2 free3
            ss_done mean_done root_done r_done diag_done bcast_done rb_done
            rot_in roped tables_in v_turned v_taken kc_in kc_turned kc_taken sc_in sc_turned sc_taken
            vc_in q_packed cur_taken qk_hi qk_lo scores_done scores_taken negm_done exp_done probs_ready
            p_turned pt_taken pv_done o_taken dcache_done dcache_taken
            gate_out sum_ready hi_out mix_split mid_split out_split sig_out sq_out acc_done
            tail_ready tail_turned tail_taken tail_out p_in p_turned2 p_hi p_lo pad_ready
            gf_in y_turned y_ready y_out cache_out dve_step pool_step""".split()
        S = {n: ctx.enter_context(nc.semaphore(n)) for n in names}
        const_made, consts_in = S["const_made"], S["consts_in"]
        loaded = [S["loaded0"], S["loaded1"]]
        free = [S[f"free{i}"] for i in range(4)]
        x_in = [ctx.enter_context(nc.semaphore(f"x_in{b}")) for b in range(NB + 1)]
        group_done, w_hi, w_lo, w_used, w_scaled = (S[n] for n in ("group_done", "w_hi", "w_lo", "w_used", "w_scaled"))

        def cols(c):
            return slice(c * CH, (c + 1) * CH)

        def xblock(b):
            return (b * P, P) if b < NB else (SEQ, NS)

        block = ctx.enter_context(nc.Block())

        @block.sync
        def _(sp):
            for l in range(DEPTH):
                for f in range(FT):
                    w = l * FT + f
                    s = w % 2
                    if w == 1:
                        for b in range(0, 4, 2):
                            sp.dma_start(xnat[:, b, :], x_prompt[0, b * P:(b + 1) * P, :]).then_inc(x_in[b], 16)
                    if w == 2:
                        for b in range(4, NB, 2):
                            sp.dma_start(xnat[:, b, :], x_prompt[0, b * P:(b + 1) * P, :]).then_inc(x_in[b], 16)
                        sp.dma_start(xnat[P - NS:P, NB, :], x_sample.rearrange("b s d -> (b s) d")).then_inc(x_in[NB], 16)
                    if w >= 2:
                        sp.wait_ge(w_lo, w - 1)
                        sp.wait_ge(w_hi, w - 1)
                    if f < NA:
                        kind, j, c0 = A_TILES[f]
                        src = w_in[l].rearrange("(k p) n -> p k n", p=P)
                        if kind in ("q", "ga"):
                            for i in range(2):
                                c = c0 + (j + 4 * i) * HD
                                sp.dma_start(stage[:, s, 0:KT, i * HD:(i + 1) * HD],
                                             src[:, :, c:c + HD]).then_inc(loaded[s], 16)
                        else:
                            c = c0 + j * P
                            sp.dma_start(stage[:, s, 0:KT, :], src[:, :, c:c + P]).then_inc(loaded[s], 16)
                    elif f < NA + KT:
                        c = (f - NA) * P
                        for i in range(2):
                            sp.dma_start(stage[i * HD:(i + 1) * HD, s, 0:4, :],
                                         w_out[l, i * 4 * HD:(i + 1) * 4 * HD, c:c + P]
                                         .rearrange("(t p) n -> p t n", p=HD)).then_inc(loaded[s], 16)
                        sp.dma_start(stage[:, s, 4:8, :], w_out[l, AW:D, c:c + P]
                                     .rearrange("(t p) n -> p t n", p=P)).then_inc(loaded[s], 16)
                    else:
                        c = (f - NA - KT) * P
                        sp.dma_start(stage[:, s, 0:KT, :], w_pg[l, :, c:c + P]
                                     .rearrange("(t p) n -> p t n", p=P)).then_inc(loaded[s], 16)
                        sp.dma_start(stage[:, s, KT:KT + KP, :], w_pp[l, :, c:c + P]
                                     .rearrange("(t p) n -> p t n", p=P)).then_inc(loaded[s], 16)
                    if w == 2:
                        with nc.allow_non_contiguous_dma("a few small vectors, one value to a partition"):
                            for i in range(DEPTH):
                                for r in range(3):
                                    sp.dma_start(cwT[:, i, r, :], conv_w[i, r].rearrange("(k p) -> p k", p=P))\
                                      .then_inc(consts_in, 16)
                                sp.dma_start(sink[:, i, :], sinks[i:i + 1, :].to_broadcast([P, H])).then_inc(consts_in, 16)
                            sp.dma_start(dmask[:], decode_mask).then_inc(consts_in, 16)
                    if f == (1 if l else 2):
                        if l == 0:
                            sp.wait_ge(S["x_turned"], NB + 1)
                        else:
                            sp.wait_ge(group_done, l * GROUPS)
                            sp.wait_ge(S["tail_out"], 16 * NTAIL * l)
                        mx = 1 - l % 2
                        sp.dma_start(cosT[:], rope_cos).then_inc(S["tables_in"], 16)
                        sp.dma_start(sinT[:], rope_sin).then_inc(S["tables_in"], 16)
                        sp.dma_start(comb[0:2 * DB, :, :].rearrange("p a n -> p (a n)"),
                                     state_conv[l].rearrange("b r n -> (b r) n")).then_inc(S["sc_in"], 16)
                        sp.dma_start(side[mx][:], cache_k[l].rearrange("b k g d -> k b (g d)")).then_inc(S["kc_in"], 16)
                        sp.dma_start(vc[mx][:], cache_v[l].rearrange("b k g d -> k b (g d)")).then_inc(S["vc_in"], 16)
                        for new, old in ((new_k_sample, cache_k), (new_v_sample, cache_v)):
                            sp.dma_start(new[l, :, 0:WB - DS].rearrange("b k g d -> b (k g d)"),
                                         old[l, :, DS:WB].rearrange("b k g d -> b (k g d)")).then_inc(S["cache_out"], 16)
                    if NA + 1 <= f < NA + 4:
                        i = f - NA - 1
                        if i == 0:
                            sp.wait_ge(S["tail_out"], 16 * NTAIL * (l + 1))
                            sp.wait_ge(S["pt_taken"], 2 * (2 * NB + 2) * (l + 1))
                            sp.wait_ge(S["pv_done"], (2 * NB + 2) * (l + 1))
                        else:
                            sp.wait_ge(S["p_turned2"], 3 * l + i)
                        if i < 2:
                            sp.dma_start(pn[:], p_prompt[l, 0, i * 4 * P:(i + 1) * 4 * P, :]
                                         .rearrange("(b p) n -> p b n", p=P)).then_inc(S["p_in"], 16)
                        else:
                            sp.dma_start(pn[0:NS, 0, :], p_sample[l].rearrange("b s n -> (b s) n"))\
                              .then_inc(S["p_in"], 16)
            sp.wait_ge(S["p_turned2"], 3 * DEPTH)
            sp.dma_start(gfb, g_final.rearrange("(a n) -> a n", a=1).to_broadcast([P, D])).then_inc(S["gf_in"], 16)
            for b in range(NB + 1):
                sp.wait_ge(S["y_ready"], b + 1)
                if b < NB:
                    sp.dma_start(y_prompt[0, b * P:(b + 1) * P, :], xnat[:, b, :]).then_inc(S["y_out"], 16)
                else:
                    sp.dma_start(y_sample.rearrange("b s d -> (b s) d"), xnat[P - NS:P, b, :]).then_inc(S["y_out"], 16)
            sp.wait_ge(S["y_out"], 16 * (NB + 1))
            sp.wait_ge(S["cache_out"], 16 * 2 * DEPTH)
            sp.wait_ge(S["tail_out"], 16 * NTAIL * DEPTH)

        @block.gpsimd
        def _(pool):
            pool.memset(ident[:], 0.0).then_inc(S["pool_step"], 1)
            pool.memset(prev_mask[:], 1.0).then_inc(S["pool_step"], 1)
            pool.memset(cur_maskT[:], 1.0).then_inc(S["pool_step"], 1)
            pool.wait_ge(S["pool_step"], 3)
            pool.affine_select(out=ident[:], in_=ident[:], compare_op=ALU.not_equal, fill=1.0, base=0,
                               pattern=[[-1, P]], channel_multiplier=1).then_inc(const_made, 1)
            pool.affine_select(out=prev_mask[:], in_=prev_mask[:], compare_op=ALU.is_gt, fill=0.0, base=0,
                               pattern=[[1, P]], channel_multiplier=-1).then_inc(const_made, 1)
            pool.affine_select(out=cur_maskT[:], in_=cur_maskT[:], compare_op=ALU.is_ge, fill=0.0, base=0,
                               pattern=[[1, P]], channel_multiplier=-1).then_inc(const_made, 1)
            pool.memset(ones[:], 1.0).then_inc(const_made, 1)
            pool.memset(neg[:], NEG).then_inc(const_made, 1)
            pool.memset(nr[:, 6, NB:NB + 1], 1.0).then_inc(const_made, 1)
            pool.wait_ge(S["g_in"], 16)
            for l in range(DEPTH):
                for f in range(FT):
                    w = l * FT + f
                    s = w % 2
                    n = KT if f < NA + KT else KT + KP
                    pool.wait_ge(loaded[s], loaded_count(w))
                    if f < NA:
                        nc.gpsimd.tensor_tensor(stage[:, s, 0:n, :], stage[:, s, 0:n, :],
                                                gT[:, l, :].rearrange("p (k a) -> p k a", a=1).to_broadcast([P, n, P]),
                                                ALU.mult).then_inc(w_scaled, 1)
                    pool.wait_ge(w_hi, w + 1)
                    nc.gpsimd.tensor_tensor(ws[:, s, 1, 0:n, :], stage[:, s, 0:n, :],
                                            ws[:, s, 0, 0:n, :].bitcast(F32), ALU.subtract).then_inc(w_lo, 1)

        @block.tensor
        def _(pe):
            def group(g, w, x, tiles, cs, waits=None, last=None):
                out = ring[:, g % 4, 0:CH]
                if g >= 4:
                    pe.wait_ge(free[g % 4], g // 4)
                n = len(tiles)
                for i, (kw, kx) in enumerate(tiles):
                    if waits:
                        pe.wait_ge(*waits(i))
                    for wp, xp in ((0, 0), (0, 1), (1, 0)):
                        mm = nc.tensor.matmul(out, ws[:, w % 2, wp, kw, :], x[:, xp, kx, cs],
                                              start=(i == 0 and wp == 0 and xp == 0), stop=(i == n - 1 and wp == 1))
                mm.then_inc(group_done, 1)

            def attention(l, step, u):
                b, g = u // 2, u % 2
                mx = 1 - l % 2
                U = l * (2 * NB + 2) + u
                rows = slice(g * HD, (g + 1) * HD)
                qp = qps[mx]
                if step == "scores":
                    if u == 0:
                        pe.wait_ge(S["roped"], 5 * (l + 1))
                        pe.wait_ge(S["kc_taken"], l + 1)
                        pe.wait_ge(S["sc_taken"], l + 1)
                    else:
                        pe.wait_ge(S["scores_taken"], U)
                    n = l * 2 * NB + u + 1
                    pe.wait_ge(S["qk_hi"], 3 * n)
                    pe.wait_ge(S["qk_lo"], 3 * n)
                    keys = slice(0, P if b == 0 else 2 * P)
                    for t in range(G):
                        for part in range(2):
                            mm = nc.tensor.matmul(pS4[:, t, keys], qst[:, g, t, :], kst[:, g, part, keys],
                                                  start=(part == 0), stop=(part == 1))
                    mm.then_inc(S["scores_done"], 1)
                elif step == "dcache":
                    pe.wait_ge(S["q_packed"], l + 1)
                    pe.wait_ge(S["scores_taken"], U)
                    for i in range(DB):
                        mm = nc.tensor.matmul(pS[:, i * G * DS:(i + 1) * G * DS], kcT[mx][rows, i, :],
                                              qp[rows, i, :, :].rearrange("p a b -> p (a b)"), start=True, stop=True)
                    mm.then_inc(S["dcache_done"], 1)
                elif step == "dscores":
                    pe.wait_ge(S["dcache_taken"], 2 * l + g + 1)
                    nc.tensor.transpose(pS[:, 512:512 + P], skt, ident[:])
                    mm = nc.tensor.matmul(pS[:, 512 + P:512 + P + NS], qp[rows].rearrange("p a b c -> p (a b c)"),
                                          kT[rows, SEQ:T], start=True, stop=True)
                    mm.then_inc(S["scores_done"], 1)
                elif step == "turn":
                    pe.wait_ge(S["probs_ready"], U + 1)
                    if b < NB:
                        for t in range(4):
                            mm = nc.tensor.transpose(pT1[:, t * P:(t + 1) * P], comb[:, t, :], ident[:])
                    else:
                        flat = comb[:].rearrange("p a n -> p (a n)")
                        nc.tensor.transpose(pT1[:, 0:P], flat[:, 0:P], ident[:])
                        mm = nc.tensor.transpose(pT1[0:NS, P:2 * P], flat[:, P:P + NS], ident[:])
                    mm.then_inc(S["p_turned"], 1)
                elif step == "pv":
                    pe.wait_ge(S["pt_taken"], 2 * (U + 1))
                    if g == 0 and b > 0:
                        pe.wait_ge(S["o_taken"], l * (NB + 1) + b)
                    if b < NB:
                        mm = nc.tensor.matmul(pO[rows, :], vnat[:, b, rows], ptcp[:, 0, :], start=True, stop=(b == 0))
                        if b:
                            mm = nc.tensor.matmul(pO[rows, :], vnat[:, b - 1, rows], ptcp[:, 1, :], start=False, stop=True)
                    else:
                        pe.wait_ge(S["vc_in"], 16 * (l + 1))
                        nc.tensor.matmul(pO[rows, 0:P], vnat[0:NS, NB, rows], ptcp[0:NS, 1, 0:P], start=True, stop=False,
                                         skip_group_check=True)
                        for i in range(DB):
                            r = slice(i * G * DS, (i + 1) * G * DS)
                            mm = nc.tensor.matmul(pO[rows, r], vc[mx][:, i, rows], ptcp[:, 0, r], start=False,
                                                  stop=(i == DB - 1), skip_group_check=True)
                    mm.then_inc(S["pv_done"], 1)

            def norm_sums(acc_ready):
                pe.wait_ge(*acc_ready)
                for b in range(NB + 1):
                    t0 = b * P if b < NB else LASTB
                    mm = nc.tensor.matmul(pT1[:, b:b + 1], acc[:, t0:t0 + P], ones[:, 0:1], start=True, stop=True)
                mm.then_inc(S["ss_done"], 1)

            def broadcast(l):
                pe.wait_ge(S["diag_done"], l + 1)
                for b in range(NB):
                    nc.tensor.matmul(pS[:, b * P:(b + 1) * P], ones[:], diag[:, b, :], start=True, stop=True)
                mm = nc.tensor.matmul(pO[:, 0:P], ones[:], diag[:, NB, :], start=True, stop=True)
                mm.then_inc(S["bcast_done"], 1)

            def turn_x(b):
                n = xblock(b)[1]
                pe.wait_ge(x_in[b], 16)
                if b >= 2:
                    pe.wait_ge(S["x_lo"], b - 1)
                for k in range(KT):
                    mm = nc.tensor.transpose(aux[:, 2 * (b % 2) + k // 4, (k % 4) * P:(k % 4) * P + n],
                                             xnat[P - n:P, b, k * P:(k + 1) * P], ident[P - n:P, P - n:P])
                mm.then_inc(S["x_turned"], 1)

            pe.wait_ge(const_made, 6)
            for l in range(DEPTH):
                xa, mx = act[l % 2], act[1 - l % 2]
                m = 1 - l % 2
                g0 = l * GROUPS
                for f in range(NA):
                    w = l * FT + f
                    for c in range(NCH):
                        s = NCH * f + c
                        if l == 0 and f == 0:
                            for b in range(3 * c + 2 if c else 0, min(3 * c + 5, NB + 1)):
                                turn_x(b)
                            pe.wait_ge(S["x_lo"], 3 * c + 3)
                        pe.wait_ge(w_lo, w + 1)
                        waits = None
                        if l and f == 0:
                            waits = lambda i, c=c: (S["out_split"], (l - 1) * B_SLOTS + NCH * i + c + 1)
                        group(g0 + s, w, xa, [(k, k) for k in range(KT)], cols(c), waits)
                        if s == 0 and l:
                            norm_sums((S["acc_done"], l * NSQ))
                        if s == BCAST[min(l, 1)]:
                            broadcast(l)
                        if s == V_TURN:
                            for g in range(g0, g0 + NCH):
                                pe.wait_ge(free[g % 4], uses(g % 4, g + 1))
                            pe.wait_ge(S["rb_done"], 2 * (l + 1))
                            for b in range(NB):
                                nc.tensor.transpose(pS[:, b * P:(b + 1) * P], rot[m][:, b * P:(b + 1) * P], ident[:])
                            mm = nc.tensor.transpose(pO[0:NS, 0:P], rot[m][:, SEQ:T], ident[:])
                            mm.then_inc(S["v_turned"], 1)
                        if s == KC_TURN:
                            pe.wait_ge(S["kc_in"], 16 * (l + 1))
                            pe.wait_ge(S["v_taken"], 2 * (l + 1))
                            for b in range(DB):
                                mm = nc.tensor.transpose(pS[:, b * P:(b + 1) * P], side[m][:, b, :], ident[:])
                            mm.then_inc(S["kc_turned"], 1)
                        if s == SC_TURN:
                            pe.wait_ge(S["sc_in"], 16 * (l + 1))
                            for j in range(4):
                                mm = nc.tensor.transpose(pO[:, j * 2 * DB:(j + 1) * 2 * DB], comb[0:2 * DB, j, :],
                                                         ident[0:2 * DB, 0:2 * DB])
                            mm.then_inc(S["sc_turned"], 1)
                        for step, u in units_at(s):
                            attention(l, step, u)
                        if s == TAILS:
                            pe.wait_ge(S["tail_ready"], 4 * (l + 1))
                            pe.wait_ge(S["scores_taken"], (2 * NB + 2) * (l + 1))
                            for j in range(4):
                                nc.tensor.transpose(pS[0:2 + NS, j * P:(j + 1) * P], utail[:, j, :], ident[:])
                            nc.tensor.transpose(pS[:, 512:512 + P], kT[:, SEQ - P:SEQ], ident[:])
                            mm = nc.tensor.transpose(pS[0:NS, 640:640 + P], kT[:, SEQ:T], ident[:])
                            mm.then_inc(S["tail_turned"], 1)
                g0 += A_SLOTS
                for f in range(KT):
                    w = l * FT + NA + f
                    pe.wait_ge(w_lo, w + 1)
                    for c in range(NCH):
                        waits = None
                        if f == 0:
                            waits = lambda i, c=c: (S["mix_split"], l * B_SLOTS + NCH * i + c + 1)
                        group(g0 + NCH * f + c, w, mx, [(k, k) for k in (4, 5, 6, 7, 0, 1, 2, 3)], cols(c), waits)
                        if c == 0 and 2 <= f < 5:
                            i = f - 2
                            pe.wait_ge(S["p_in"], 16 * (3 * l + i + 1))
                            if i == 0:
                                pe.wait_ge(S["tail_taken"], 3 * (l + 1))
                            else:
                                pe.wait_ge(S["p_hi"], 3 * l + i)
                                pe.wait_ge(S["p_lo"], 3 * l + i)
                            for k in range(KP):
                                for b in range(4 if i < 2 else 1):
                                    n = P if i < 2 else NS
                                    mm = nc.tensor.transpose(pS[:, k * 512 + b * P:k * 512 + b * P + n],
                                                             pn[0:n, b, k * P:(k + 1) * P], ident[0:n, 0:n])
                            mm.then_inc(S["p_turned2"], 1)
                g0 += B_SLOTS
                for f in range(KT):
                    w = l * FT + NA + KT + f
                    pe.wait_ge(w_lo, w + 1)
                    for c in range(NCH):
                        s = NCH * f + c
                        if s == 0:
                            pe.wait_ge(S["p_hi"], 3 * (l + 1))
                            pe.wait_ge(S["p_lo"], 3 * (l + 1))
                        group(g0 + 2 * s, w, pT, [(KT + k, k) for k in range(KP)], cols(c))
                        waits = None
                        if f == 0:
                            waits = lambda i, c=c: (S["mid_split"], l * B_SLOTS + NCH * i + c + 1)
                        group(g0 + 2 * s + 1, w, xa, [(k, k) for k in range(KT)], cols(c), waits)
            norm_sums((S["acc_done"], DEPTH * NSQ))
            pe.wait_ge(S["out_split"], DEPTH * B_SLOTS)
            for i in range(4):
                pe.wait_ge(free[i], uses(i, DEPTH * GROUPS))
            for b in range(NB + 1):
                t0 = b * P if b < NB else LASTB
                if b >= 2:
                    pe.wait_ge(S["y_ready"], b - 1)
                for k in range(KT):
                    mm = nc.tensor.transpose(ring[:, 2 * (b % 2) + k // 4, (k % 4) * P:(k % 4 + 1) * P],
                                             xfin[:, k, t0:t0 + P], ident[:])
                mm.then_inc(S["y_turned"], 1)

        @block.scalar
        def _(sc):
            def split_weights(w):
                f = w % FT
                n = KT if f < NA + KT else KT + KP
                if f < NA:
                    sc.wait_ge(w_scaled, (w // FT) * NA + f + 1)
                else:
                    sc.wait_ge(loaded[w % 2], loaded_count(w))
                if w >= 2:
                    sc.wait_ge(group_done, last_group(w - 2) + 1)
                    sc.wait_ge(w_lo, w - 1)
                nc.scalar.activation(ws[:, w % 2, 0, 0:n, :], stage[:, w % 2, 0:n, :], ACT.Copy).then_inc(w_hi, 1)

            def bank(g):
                sc.wait_ge(group_done, g + 1)
                return ring[:, g % 4, 0:CH]

            def high(dst, s, ready):
                sc.wait_ge(*ready)
                nc.scalar.activation(dst, tmp[:, s % 2, :], ACT.Copy).then_inc(S["hi_out"], 1)

            with nc.allow_non_contiguous_dma("a few small vectors, one value to a partition"):
                sc.dma_start(gT[:, 0:DEPTH, :], g_norm.rearrange("l (k p) -> p l k", p=P)).then_inc(S["g_in"], 16)
                for b in range(1, NB, 2):
                    sc.dma_start(xnat[:, b, :], x_prompt[0, b * P:(b + 1) * P, :]).then_inc(x_in[b], 16)
            def square_x(b):
                r0 = P - xblock(b)[1]
                if b == NB:
                    sc.wait_ge(const_made, 6)
                if b:
                    sc.wait_ge(S["x_sq"], b)
                nc.scalar.activation(diag[r0:P, 0:KT, :].rearrange("p a n -> p (a n)"), xnat[r0:P, b, :], ACT.Square,
                                     accum_out=nr[r0:P, 6, b:b + 1]).then_inc(S["x_sq"], 1)

            for b in range(NB + 1):
                t0, n = xblock(b)
                sc.wait_ge(S["x_turned"], b + 1)
                src = aux[:, 2 * (b % 2):2 * (b % 2) + 2, :].rearrange("p a (k n) -> p (a k) n", n=P)[:, :, 0:n]
                nc.scalar.activation(act[0][:, 0, :, t0:t0 + n], src, ACT.Copy).then_inc(S["x_hi"], 1)
                if b == 0:
                    split_weights(0)
                else:
                    square_x(b - 1)
                if b == 6:
                    split_weights(1)
            square_x(NB)

            sums = 0
            for l in range(DEPTH):
                xa, mx = act[l % 2], act[1 - l % 2]
                m = 1 - l % 2
                g0 = l * GROUPS
                for s in range(A_SLOTS):
                    f, c = s // NCH, s % NCH
                    w = l * FT + f
                    kind, j, _ = A_TILES[f]
                    g = g0 + s
                    freed = (free[g % 4], uses(g % 4, g + 1))
                    if c == 0 and w >= 1:
                        split_weights(w + 1)
                    if s and A_TILES[(s - 1) // NCH][0] == "ga":
                        sums += 1
                        high(mx[:, 0, A_TILES[(s - 1) // NCH][1], cols((s - 1) % NCH)], s, (S["sum_ready"], sums))
                    if s == 0:
                        sc.wait_ge(S["mean_done"], l + 1)
                        nc.scalar.activation(nr[:, 1, :], nr[:, 0, :], ACT.Sqrt).then_inc(S["root_done"], 1)
                    if s == BCAST[min(l, 1)]:
                        sc.wait_ge(S["bcast_done"], l + 1)
                        nc.scalar.activation(rb[:, 0:SEQ], pS, ACT.Copy).then_inc(S["rb_done"], 1)
                        nc.scalar.activation(rb[:, SEQ:T], pO[:, P - NS:P], ACT.Copy).then_inc(S["rb_done"], 1)
                    if s == V_TURN:
                        sc.wait_ge(S["v_turned"], l + 1)
                        nc.scalar.activation(vnat[:, 0:NB, :], pS.rearrange("p (b n) -> p b n", n=P), ACT.Copy)\
                          .then_inc(S["v_taken"], 1)
                        nc.scalar.activation(vnat[0:NS, NB, :], pO[0:NS, 0:P], ACT.Copy).then_inc(S["v_taken"], 1)
                    if s == KC_TURN:
                        sc.wait_ge(S["kc_turned"], l + 1)
                        nc.scalar.activation(kcT[m][:], pS.rearrange("p (b n) -> p b n", n=P), ACT.Copy)\
                          .then_inc(S["kc_taken"], 1)
                    if s == SC_TURN:
                        sc.wait_ge(S["sc_turned"], l + 1)
                        nc.scalar.activation(scT[:], pO[:, 0:8 * DB].rearrange("p (j n) -> p j n", j=4), ACT.Copy)\
                          .then_inc(S["sc_taken"], 1)
                    if 1 <= f < 6 and c == NCH - 1:
                        i = f - 1
                        for h in range(g - NCH + 1, g + 1):
                            sc.wait_ge(free[h % 4], uses(h % 4, h + 1))
                        if i == 0:
                            sc.wait_ge(S["v_turned"], l + 1)
                        else:
                            sc.wait_ge(S["roped"], 5 * l + i)
                        src = kT[:] if i == 0 else raw[m][:, i - 1, :]
                        for a in range(4):
                            o = a ^ 1
                            sc.dma_start(rot[m][32 * a:32 * a + 32, :], src[32 * o:32 * o + 32, :])\
                              .then_inc(S["rot_in"], 16)
                    if kind in ("gc", "ga"):
                        sc.wait_ge(*freed)
                        nc.scalar.activation(gate[:, s % 2, :], gate[:, s % 2, :], ACT.Silu).then_inc(S["gate_out"], 1)
                    for step, u in units_at(s):
                        b, gg = u // 2, u % 2
                        U = l * (2 * NB + 2) + u
                        own, other = slice(gg * HD, (gg + 1) * HD), slice((1 - gg) * HD, (2 - gg) * HD)
                        if step == "split":
                            if u < 2:
                                sc.wait_ge(S["roped"], 5 * (l + 1))
                            else:
                                sc.wait_ge(S["scores_done"], U - 1)
                            tok = slice(b * P, (b + 1) * P)
                            key = slice(b % 2 * P, (b % 2 + 1) * P)
                            nc.scalar.activation(qst[own, gg, :, :], raw[m][own, :, tok], ACT.Copy).then_inc(S["qk_hi"], 1)
                            nc.scalar.activation(kst[own, gg, 0, key], kT[own, tok], ACT.Copy).then_inc(S["qk_hi"], 1)
                            nc.scalar.activation(kst[other, gg, 0, key], kT[own, tok], ACT.Copy).then_inc(S["qk_hi"], 1)
                        elif step == "scores":
                            sc.wait_ge(S["scores_done"], U + 1)
                            nc.scalar.activation(comb[:], pS4[:, :, b % 2 * P:(b % 2 + 1) * P], ACT.Copy).then_inc(S["cur_taken"], 1)
                        elif step == "dcache":
                            sc.wait_ge(S["dcache_done"], 2 * l + gg + 1)
                            nc.scalar.activation(skt, pS[:, 0:P], ACT.Copy).then_inc(S["dcache_taken"], 1)
                        elif step == "pv" and gg == 1:
                            sc.wait_ge(S["pv_done"], U + 1)
                            if b < NB:
                                nc.scalar.activation(raw[m][:, :, b * P:(b + 1) * P],
                                                     pO.rearrange("p (t n) -> p t n", t=4), ACT.Copy)\
                                  .then_inc(S["o_taken"], 1)
                            else:
                                nc.scalar.activation(raw[m][:, :, SEQ:T].rearrange("p h (b s) -> p b h s", s=DS),
                                                     pO[:, 0:P].rearrange("p (b h s) -> p b h s", h=G, s=DS), ACT.Copy)\
                                  .then_inc(S["o_taken"], 1)
                        if step in ("scores", "dscores"):
                            sc.wait_ge(S["negm_done"], 2 * (U + 1))
                            if b < NB:
                                for t in range(4):
                                    nc.scalar.activation(comb[:, t, :], comb[:, t, :], ACT.Exp, bias=st[:, 1, t:t + 1],
                                                         scale=SCALE, accum_out=st[:, 4, t:t + 1]).then_inc(S["exp_done"], 1)
                                nc.scalar.activation(st[:, 3, :], st[:, 2, :], ACT.Exp).then_inc(S["exp_done"], 1)
                            else:
                                flat = comb[:].rearrange("p a n -> p (a n)")[:, 0:P + NS]
                                nc.scalar.activation(flat, flat, ACT.Exp, bias=st[:, 1, 0:1], scale=SCALE,
                                                     accum_out=st[:, 4, 0:1]).then_inc(S["exp_done"], 1)
                                nc.scalar.activation(st[:, 3, 0:1], st[:, 2, 0:1], ACT.Exp).then_inc(S["exp_done"], 1)
                    if kind == "bg":
                        high(mx[:, 0, 4 + j, cols(c)], s, freed)
                    if s == TAILS:
                        sc.wait_ge(S["tail_turned"], l + 1)
                        ctail = comb[:].rearrange("p a n -> p (a n)")[0:2 + NS, :]
                        nc.scalar.activation(ctail, pS[0:2 + NS, 0:512], ACT.Copy).then_inc(S["tail_taken"], 1)
                        nc.scalar.activation(ptcp[:, 0, 0:P], pS[:, 512:512 + P], ACT.Copy).then_inc(S["tail_taken"], 1)
                        nc.scalar.activation(ptcp[0:NS, 0, P:2 * P], pS[0:NS, 640:640 + P], ACT.Copy)\
                          .then_inc(S["tail_taken"], 1)
                        sc.wait_ge(S["tail_taken"], 3 * (l + 1))
                        out = S["tail_out"]
                        sc.dma_start(new_conv_prompt[l, 0], ctail[0:2, :]).then_inc(out, 16)
                        for r in range(2):
                            o = 2 + DS - 2 + r
                            sc.dma_start(new_conv_sample[l, :, r, :], ctail[o:o + DS * (DB - 1) + 1:DS, :]).then_inc(out, 16)
                        sc.dma_start(new_k_prompt[l, 0].rearrange("k g d -> k (g d)"), ptcp[:, 0, 0:P]).then_inc(out, 16)
                        sc.dma_start(new_v_prompt[l, 0].rearrange("k g d -> k (g d)"), vnat[:, NB - 1, :]).then_inc(out, 16)
                        for r in range(DS):
                            sc.dma_start(new_k_sample[l, :, WB - DS + r].rearrange("b g d -> b (g d)"),
                                         ptcp[r:r + DS * (DB - 1) + 1:DS, 0, P:2 * P]).then_inc(out, 16)
                            sc.dma_start(new_v_sample[l, :, WB - DS + r].rearrange("b g d -> b (g d)"),
                                         vnat[r:r + DS * (DB - 1) + 1:DS, NB, :]).then_inc(out, 16)
                sums += 1
                high(mx[:, 0, 3, cols(NCH - 1)], A_SLOTS, (S["sum_ready"], sums))
                g0 += A_SLOTS
                for s in range(B_SLOTS):
                    f, c = s // NCH, s % NCH
                    if c == 0:
                        split_weights(l * FT + NA + f + 1)
                    sums += 1
                    high(xa[:, 0, f, cols(c)], s, (S["sum_ready"], sums))
                    if c == 0 and 2 <= f < 5:
                        i = f - 2
                        sc.wait_ge(S["p_turned2"], 3 * l + i + 1)
                        t0, n = (i * 512, 512) if i < 2 else (SEQ, NS)
                        if i == 0:
                            sc.wait_ge(S["tail_out"], 16 * NTAIL * (l + 1))
                        nc.scalar.activation(pT[:, 0, :, t0:t0 + n], pS.rearrange("p (k n) -> p k n", k=KP)[:, :, 0:n],
                                             ACT.Copy).then_inc(S["p_hi"], 1)
                g0 += B_SLOTS
                for s in range(B_SLOTS):
                    f, c = s // NCH, s % NCH
                    w = l * FT + NA + KT + f
                    if c == 0 and w + 1 < DEPTH * FT:
                        split_weights(w + 1)
                    g = g0 + 2 * s + 1
                    src = bank(g)
                    if s >= 2:
                        sc.wait_ge(free[(g - 5) % 4], uses((g - 5) % 4, g - 4))
                    nc.scalar.activation(gate[:, s % 2, :], src, ACT.Sigmoid).then_inc(free[g % 4], 1)
                    if l < DEPTH - 1:
                        sums += 1
                        high(mx[:, 0, f, cols(c)], s, (S["sum_ready"], sums))
                        last = tmp[:, s % 2, :]
                    else:
                        sc.wait_ge(S["out_split"], l * B_SLOTS + s + 1)
                        last = xfin[:, f, cols(c)]
                    if s >= 2 * NCH:
                        sc.wait_ge(S["acc_done"], l * NSQ + s - 2 * NCH + 1)
                    nc.scalar.activation(acc[:, cols(c)] if f == 0 else ytmp[:, c, :], last, ACT.Square)\
                      .then_inc(S["sq_out"], 1)
            sc.wait_ge(S["mean_done"], DEPTH + 1)
            nc.scalar.activation(nr[:, 1, :], nr[:, 0, :], ACT.Sqrt).then_inc(S["root_done"], 1)

        @block.vector
        def _(ve):
            V = nc.vector
            steps = [0]

            def link(ins):
                steps[0] += 1
                ins.then_inc(S["dve_step"], 1)
                ve.wait_ge(S["dve_step"], steps[0])

            def norm_scale(n):
                if n:
                    ve.wait_ge(S["ss_done"], n)
                    sums = pT1[:, 0:NB + 1]
                else:
                    ve.wait_ge(S["x_sq"], NB + 1)
                    sums = nr[:, 6, :]
                V.tensor_scalar(nr[:, 0, :], sums, 1.0 / D, EPS, ALU.mult, ALU.add).then_inc(S["mean_done"], 1)
                ve.wait_ge(S["root_done"], n + 1)
                link(V.reciprocal(nr[:, 2, :], nr[:, 1, :]))
                link(V.tensor_tensor(nr[:, 3, :], nr[:, 2, :], nr[:, 2, :], ALU.mult))
                link(V.tensor_tensor(nr[:, 4, :], nr[:, 3, :], nr[:, 0, :], ALU.mult))
                link(V.tensor_scalar(nr[:, 3, :], nr[:, 4, :], -0.5, 1.5, ALU.mult, ALU.add))
                link(V.tensor_tensor(nr[:, 5, :], nr[:, 3, :], nr[:, 2, :], ALU.mult))

            def bank(g):
                ve.wait_ge(group_done, g + 1)
                return ring[:, g % 4, 0:CH]

            highs = [0]

            def low(x, t, c, s, done):
                dst, hi = x[:, 1, t, cols(c)], x[:, 0, t, cols(c)]
                highs[0] += 1
                ve.wait_ge(S["hi_out"], highs[0])
                V.tensor_tensor(dst, tmp[:, s % 2, :], hi.bitcast(F32), ALU.subtract).then_inc(done, 1)

            ve.wait_ge(const_made, 6)
            for b in range(NB + 1):
                t0, n = xblock(b)
                ve.wait_ge(S["x_hi"], b + 1)
                src = aux[:, 2 * (b % 2):2 * (b % 2) + 2, :].rearrange("p a (k n) -> p (a k) n", n=P)[:, :, 0:n]
                V.tensor_tensor(act[0][:, 1, :, t0:t0 + n], src, act[0][:, 0, :, t0:t0 + n].bitcast(F32),
                                ALU.subtract).then_inc(S["x_lo"], 1)

            def add_squares(l, s):
                f, c = s // NCH, s % NCH
                ve.wait_ge(S["sq_out"], l * B_SLOTS + s + 1)
                if f == 0:
                    return
                if f >= 2:
                    ve.wait_ge(S["acc_done"], l * NSQ + s - 2 * NCH + 1)
                V.tensor_tensor(acc[:, cols(c)], acc[:, cols(c)], ytmp[:, c, :], ALU.add).then_inc(S["acc_done"], 1)

            for l in range(DEPTH):
                xa, mx = act[l % 2], act[1 - l % 2]
                m = 1 - l % 2
                g0 = l * GROUPS
                norm_scale(l)
                V.tensor_tensor(diag[:], ident[:].rearrange("p (a n) -> p a n", a=1).to_broadcast([P, NB + 1, P]),
                                     nr[:, 5, :].rearrange("p (b a) -> p b a", a=1).to_broadcast([P, NB + 1, P]),
                                     ALU.mult).then_inc(S["diag_done"], 1)
                if l == 0:
                    ve.wait_ge(consts_in, CONSTS)
                    link(V.tensor_scalar(nsink[:, :, 0:H], sink[:], -1.0, None, ALU.mult))
                    pick = st[:, 0:2 * DEPTH, :]
                    link(V.tensor_tensor(pick, sink[:].rearrange("p l (g h) -> p (l g) h", h=G),
                                         dmask[:, P + NS:].rearrange("p (a h) -> p a h", a=1).to_broadcast([P, 2 * DEPTH, G]),
                                         ALU.mult))
                    link(V.tensor_reduce(sinkd[:].rearrange("p l g -> p (l g)"), pick, AX.X, ALU.add))
                    link(V.tensor_scalar(nsink[:, :, H:H + 2], sinkd[:], -1.0, None, ALU.mult))
                ve.wait_ge(S["rb_done"], 2 * (l + 1))
                link(V.memset(up[:, 0:2], 0.0))

                def behind(s):
                    if s >= 2 and A_TILES[(s - 2) // NCH][0] == "ga":
                        low(mx, A_TILES[(s - 2) // NCH][1], (s - 2) % NCH, s - 1, S["mix_split"])
                    if not s or s > A_SLOTS:
                        return
                    kind, j, _ = A_TILES[(s - 1) // NCH]
                    c = (s - 1) % NCH
                    gt = gate[:, (s - 1) % 2, :]
                    if kind == "bg":
                        low(mx, 4 + j, c, s - 1, S["mix_split"])
                    elif kind == "gc":
                        ve.wait_ge(S["gate_out"], gates(l, kind, j, c))
                        link(V.tensor_tensor(ytmp[:, c, :], ytmp[:, c, :], gt, ALU.mult))
                    elif kind == "ga":
                        ve.wait_ge(S["gate_out"], gates(l, kind, j, c))
                        ve.wait_ge(S["o_taken"], (l + 1) * (NB + 1))
                        V.tensor_tensor(tmp[:, s % 2, :], gt, raw[m][:, j, cols(c)], ALU.mult).then_inc(S["sum_ready"], 1)

                for s in range(A_SLOTS):
                    f, c = s // NCH, s % NCH
                    kind, j, _ = A_TILES[f]
                    behind(s)
                    g = g0 + s
                    src = bank(g)
                    r = rb[:, cols(c)]
                    fr = free[g % 4]
                    if kind in ("v", "k", "q"):
                        dst = {"v": rot[m][:, cols(c)], "k": kT[:, cols(c)], "q": raw[m][:, j, cols(c)]}[kind]
                        V.tensor_tensor(dst, src, r, ALU.mult).then_inc(fr, 1)
                    elif kind == "cg":
                        V.tensor_tensor(ytmp[:, c, :], src, r, ALU.mult).then_inc(fr, 1)
                    elif kind == "hc":
                        t = tmp[:, s % 2, :]
                        V.tensor_tensor(t, src, r, ALU.mult).then_inc(fr, 1)
                    elif kind == "gc":
                        V.tensor_tensor(gate[:, s % 2, :], src, r, ALU.mult).then_inc(fr, 1)
                    elif kind == "bg":
                        V.tensor_tensor(tmp[:, s % 2, :], src, ytmp[:, c, :], ALU.mult).then_inc(fr, 1)
                    elif kind == "ga":
                        V.tensor_tensor(gate[:, s % 2, :], src, r, ALU.mult).then_inc(fr, 1)
                    if 2 <= f < 7 and c == 1:
                        i = f - 2
                        x = kT[:] if i == 0 else raw[m][:, i - 1, :]
                        ve.wait_ge(S["tables_in"], 32 * (l + 1))
                        ve.wait_ge(S["rot_in"], 64 * (5 * l + i + 1))
                        link(V.tensor_tensor(rot[m][:], rot[m][:], sinT[:], ALU.mult))
                        link(V.tensor_tensor(x, x, cosT[:], ALU.mult))
                        V.tensor_tensor(x, x, rot[m][:], ALU.add).then_inc(S["roped"], 1)
                    if s == QPACK:
                        ve.wait_ge(S["roped"], 5 * (l + 1))
                        V.tensor_copy(qps[m][:], raw[m][:, :, SEQ:T].rearrange("p h (b s) -> p b h s", s=DS))\
                         .then_inc(S["q_packed"], 1)
                    for step, u in units_at(s):
                        b, gg = u // 2, u % 2
                        U = l * (2 * NB + 2) + u
                        dec = b == NB
                        n = 1 if dec else 4
                        flat = comb[:].rearrange("p a n -> p (a n)")[:, 0:P + NS]
                        own, other = slice(gg * HD, (gg + 1) * HD), slice((1 - gg) * HD, (2 - gg) * HD)
                        if step == "split":
                            tok = slice(b * P, (b + 1) * P)
                            key = slice(b % 2 * P, (b % 2 + 1) * P)
                            ve.wait_ge(S["qk_hi"], 3 * (l * 2 * NB + u) + 2)
                            V.tensor_tensor(qst[other, gg, :, :], raw[m][own, :, tok], qst[own, gg, :, :].bitcast(F32),
                                            ALU.subtract).then_inc(S["qk_lo"], 1)
                            for half in (own, other):
                                V.tensor_tensor(kst[half, gg, 1, key], kT[own, tok],
                                                kst[own, gg, 0, key].bitcast(F32), ALU.subtract).then_inc(S["qk_lo"], 1)
                        elif step in ("scores", "dscores"):
                            if dec:
                                ve.wait_ge(S["scores_done"], U + 1)
                                V.tensor_tensor(flat, pS[:, 512:512 + P + NS], dmask[:, 0:P + NS], ALU.add).then_inc(S["scores_taken"], 1)
                                ve.wait_ge(S["scores_taken"], U + 1)
                                link(V.tensor_reduce(st[:, 0, 0:1], flat, AX.X, ALU.max))
                                sk, nsk = sinkd[:, l, gg:gg + 1], nsink[:, l, H + gg:H + gg + 1]
                            else:
                                ve.wait_ge(S["cur_taken"], l * 2 * NB + u + 1)
                                mask = prev_mask[:].bitcast(U32).rearrange("p (a n) -> p a n", a=1).to_broadcast([P, 4, P])
                                data = pS4[:, :, (b + 1) % 2 * P:((b + 1) % 2 + 1) * P] if b else neg[:].rearrange("p (a n) -> p a n", a=1).to_broadcast([P, 4, P])
                                V.copy_predicated(comb[:], mask, data).then_inc(S["scores_taken"], 1)
                                ve.wait_ge(S["scores_taken"], U + 1)
                                link(V.tensor_reduce(st[:, 0, :], comb[:], AX.X, ALU.max))
                                sk, nsk = sink[:, l, gg * G:(gg + 1) * G], nsink[:, l, gg * G:(gg + 1) * G]
                            V.scalar_tensor_tensor(st[:, 1, 0:n], st[:, 0, 0:n], -SCALE, nsk, ALU.mult, ALU.min)\
                             .then_inc(S["negm_done"], 1)
                            ve.wait_ge(S["negm_done"], 2 * U + 1)
                            V.tensor_tensor(st[:, 2, 0:n], st[:, 1, 0:n], sk, ALU.add).then_inc(S["negm_done"], 1)
                        elif step == "norm":
                            ve.wait_ge(S["exp_done"], exps(l, u))
                            link(V.tensor_tensor(st[:, 5, 0:n], st[:, 4, 0:n], st[:, 3, 0:n], ALU.add))
                            link(V.reciprocal(st[:, 6, 0:n], st[:, 5, 0:n]))
                            if dec:
                                V.tensor_scalar(flat, flat, st[:, 6, 0:1], None, ALU.mult).then_inc(S["probs_ready"], 1)
                            else:
                                V.tensor_tensor(comb[:], comb[:], st[:, 6, :].rearrange("p (a n) -> p a n", n=1)
                                                .to_broadcast([P, 4, P]), ALU.mult).then_inc(S["probs_ready"], 1)
                        elif step == "turn":
                            ve.wait_ge(S["p_turned"], U + 1)
                            if dec:
                                V.tensor_copy(ptcp[:, 0, 0:P], pT1[:, 0:P]).then_inc(S["pt_taken"], 1)
                                V.tensor_copy(ptcp[0:NS, 1, 0:P], pT1[0:NS, P:2 * P]).then_inc(S["pt_taken"], 1)
                            else:
                                pt = pT1.rearrange("p (a n) -> p a n", a=4)
                                V.tensor_tensor(ptcp[:, 0, :].rearrange("p (a n) -> p a n", a=4), pt,
                                                cur_maskT[:].rearrange("p (a n) -> p a n", a=1).to_broadcast([P, 4, P]),
                                                ALU.mult).then_inc(S["pt_taken"], 1)
                                ve.wait_ge(S["pt_taken"], 2 * U + 1)
                                V.tensor_tensor(ptcp[:, 1, :], pT1, ptcp[:, 0, :], ALU.subtract)\
                                 .then_inc(S["pt_taken"], 1)
                    if kind == "hc":
                        ve.wait_ge(fr, uses(g % 4, g + 1))
                        ve.wait_ge(free[(g - NCH) % 4], uses((g - NCH) % 4, g - NCH + 1))
                        n = min(CH, SEQ - c * CH)
                        link(V.tensor_tensor(up[:, 2 + c * CH:2 + c * CH + n], t[:, 0:n], ytmp[:, c, 0:n], ALU.mult))
                        w3 = [cwT[:, l, i, j:j + 1] for i in range(3)]
                        link(V.tensor_scalar(ytmp[:, c, 0:n], up[:, c * CH:c * CH + n], w3[0], None, ALU.mult))
                        for i in (1, 2):
                            link(V.scalar_tensor_tensor(ytmp[:, c, 0:n], up[:, c * CH + i:c * CH + i + n], w3[i],
                                                        ytmp[:, c, 0:n], ALU.mult, ALU.add))
                    if kind == "gc":
                        if c == 0:
                            if j == 0:
                                ve.wait_ge(S["sc_taken"], l + 1)
                            z, n = NCH - 1, SEQ - (NCH - 1) * CH
                            t = tmp[:, (s - 1) % 2, :]
                            w3 = [cwT[:, l, i, j:j + 1] for i in range(3)]
                            link(V.tensor_copy(us[:, :, 0:2], scT[:, j, :].rearrange("p (b r) -> p b r", r=2)))
                            link(V.tensor_tensor(us[:, :, 2:2 + DS], t[:, n:CH].rearrange("p (b s) -> p b s", s=DS),
                                                 ytmp[:, z, n:CH].rearrange("p (b s) -> p b s", s=DS), ALU.mult))
                            ys = ytmp[:, z, n:CH].rearrange("p (b s) -> p b s", s=DS)
                            link(V.tensor_scalar(ys, us[:, :, 0:DS], w3[0], None, ALU.mult))
                            for i in (1, 2):
                                link(V.scalar_tensor_tensor(ys, us[:, :, i:i + DS], w3[i], ys, ALU.mult, ALU.add))
                            link(V.tensor_copy(utail[:, j, 0:2], up[:, SEQ:SEQ + 2]))
                            V.tensor_copy(utail[:, j, 2:2 + NS].rearrange("p (b s) -> p b s", s=DS),
                                          us[:, :, 2:2 + DS]).then_inc(S["tail_ready"], 1)
                        link(V.tensor_tensor(ytmp[:, c, :], ytmp[:, c, :], r, ALU.mult))
                behind(A_SLOTS)
                behind(A_SLOTS + 1)
                ve.wait_ge(S["mix_split"], (l + 1) * B_SLOTS)
                g0 += A_SLOTS
                for s in range(B_SLOTS):
                    f, c = s // NCH, s % NCH
                    if s:
                        low(xa, (s - 1) // NCH, (s - 1) % NCH, s - 1, S["mid_split"])
                    g = g0 + s
                    t = tmp[:, s % 2, :]
                    V.tensor_tensor(t, bank(g), xa[:, 0, f, cols(c)].bitcast(F32), ALU.add).then_inc(free[g % 4], 1)
                    ve.wait_ge(free[g % 4], uses(g % 4, g + 1))
                    V.tensor_tensor(t, t, xa[:, 1, f, cols(c)].bitcast(F32), ALU.add).then_inc(S["sum_ready"], 1)
                    if c == 0 and 2 <= f < 5:
                        i = f - 2
                        ve.wait_ge(S["p_hi"], 3 * l + i + 1)
                        t0, n = (i * 512, 512) if i < 2 else (SEQ, NS)
                        V.tensor_tensor(pT[:, 1, :, t0:t0 + n], pS.rearrange("p (k n) -> p k n", k=KP)[:, :, 0:n],
                                        pT[:, 0, :, t0:t0 + n].bitcast(F32), ALU.subtract).then_inc(S["p_lo"], 1)
                low(xa, KT - 1, NCH - 1, B_SLOTS - 1, S["mid_split"])
                g0 += B_SLOTS
                for s in range(B_SLOTS):
                    f, c = s // NCH, s % NCH
                    if s:
                        if l < DEPTH - 1:
                            low(mx, (s - 1) // NCH, (s - 1) % NCH, s - 1, S["out_split"])
                        add_squares(l, s - 1)
                    g = g0 + 2 * s
                    src = bank(g)
                    t = tmp[:, s % 2, :]
                    ve.wait_ge(free[(g + 1) % 4], uses((g + 1) % 4, g + 2))
                    V.tensor_tensor(t, src, gate[:, s % 2, :], ALU.mult).then_inc(free[g % 4], 1)
                    ve.wait_ge(free[g % 4], uses(g % 4, g + 1))
                    link(V.tensor_tensor(t, t, xa[:, 0, f, cols(c)].bitcast(F32), ALU.add))
                    if l < DEPTH - 1:
                        V.tensor_tensor(t, t, xa[:, 1, f, cols(c)].bitcast(F32), ALU.add).then_inc(S["sum_ready"], 1)
                    else:
                        V.tensor_tensor(xfin[:, f, cols(c)], t, xa[:, 1, f, cols(c)].bitcast(F32), ALU.add)\
                         .then_inc(S["out_split"], 1)
                if l < DEPTH - 1:
                    low(mx, KT - 1, NCH - 1, B_SLOTS - 1, S["out_split"])
                add_squares(l, B_SLOTS - 1)
            norm_scale(DEPTH)
            ve.wait_ge(S["gf_in"], 16)
            for b in range(NB + 1):
                ve.wait_ge(S["y_turned"], b + 1)
                V.scalar_tensor_tensor(xnat[:, b, :], ring[:, 2 * (b % 2):2 * (b % 2) + 2, :].rearrange("p a n -> p (a n)"),
                                       nr[:, 5, b:b + 1], gfb, ALU.mult, ALU.mult).then_inc(S["y_ready"], 1)


_INS = ["x_prompt", "x_sample", "cache_k", "cache_v", "state_conv", "p_prompt", "p_sample", "g_norm", "w_in",
        "sinks", "conv_w", "w_out", "w_pg", "w_pp", "g_final"]


def _constants(seq, batch, steps, past, head_dim, group, window):
    import numpy as np

    inv = (10000.0 ** (-np.arange(0, head_dim, 2) / head_dim)).astype(np.float32)
    pos = np.concatenate([np.arange(seq), np.tile(past + np.arange(steps), batch)]).astype(np.float32)
    ang = (inv[:, None] * pos[None, :]).astype(np.float64)
    cos, sin = np.cos(ang).astype(np.float32), np.sin(ang).astype(np.float32)
    b, h, s = (a.ravel()[:, None] for a in np.indices((batch, group, steps)))
    cached = np.arange(window)[None, :] > s
    kb, ks = (a.ravel()[None, :] for a in np.indices((batch, steps)))
    new = (kb == b) & (ks <= s)
    mask = np.where(np.concatenate([cached, new], 1), 0.0, -1e30)
    flags = np.arange(group)[None, :] == h
    return (np.tile(cos, (4, 1)), np.concatenate([-sin, sin] * 2, 0),
            np.concatenate([mask, flags], 1).astype(np.float32))


def kernel(**inputs):
    import numpy as _np
    import concourse.bacc as _bacc
    from concourse import mybir as _mybir
    from concourse.bass_utils import run_bass_kernel_spmd as _run

    nc = _bacc.Bacc("TRN2", target_bir_lowering=False, num_devices=1)
    arrays, args = {}, []

    def give(name, a):
        arrays[f"in_{name}_dram"] = a
        args.append(nc.dram_tensor(f"in_{name}_dram", a.shape, _mybir.dt.from_np(a.dtype), kind="ExternalInput").ap())

    for name in _INS:
        give(name, _np.ascontiguousarray(inputs[name]))
    shape = {n: inputs[n].shape for n in _INS}
    depth, batch, window, kv, head_dim = shape["cache_k"]
    tables = _constants(shape["x_prompt"][1], batch, shape["x_sample"][1], 4096, head_dim,
                        shape["sinks"][1] // kv, window)
    for name, a in zip(("rope_cos", "rope_sin", "decode_mask"), tables):
        give(name, _np.ascontiguousarray(a))
    f32 = _mybir.dt.float32
    conv = shape["state_conv"]
    outs = [shape["x_prompt"], shape["x_sample"], (depth, 1, window, kv, head_dim), (depth, 1, window, kv, head_dim),
            (depth, 1, conv[2], conv[3]), shape["cache_k"], shape["cache_v"], conv]
    for i, s in enumerate(outs):
        args.append(nc.dram_tensor(f"out_{i}_dram", s, f32, kind="ExternalOutput").ap())
    hybrid_trunk(nc, *args)
    r = _run(nc, [arrays], core_ids=[0])
    return tuple(r.results[0][f"out_{i}_dram"] for i in range(len(outs)))
```

```python
from contextlib import ExitStack

import concourse.bass as bass
from concourse import mybir

F32 = mybir.dt.float32
F32R = mybir.dt.float32r
U32 = mybir.dt.uint32
ALU = mybir.AluOpType
ACT = mybir.ActivationFunctionType
AX = mybir.AxisListType
P = 128
NEG = -1e30
EPS = 1e-6


def hybrid_trunk(nc, x_prompt, x_sample, cache_k, cache_v, state_conv, p_prompt, p_sample, g_norm, w_in,
                 sinks, conv_w, w_out, w_pg, w_pp, g_final, rope_cos, rope_sin, decode_mask,
                 y_prompt, y_sample, new_k_prompt, new_v_prompt, new_conv_prompt,
                 new_k_sample, new_v_sample, new_conv_sample):
    DEPTH, D = g_norm.shape
    SEQ = x_prompt.shape[1]
    DB, DS, _ = x_sample.shape
    NS = DB * DS
    T = SEQ + NS
    KT = D // P
    NCH = 3
    CH = T // NCH
    NB = SEQ // P
    PLE = p_prompt.shape[3]
    KP = PLE // P
    HD = cache_k.shape[4]
    H = sinks.shape[1]
    G = H // 2
    WB = cache_k.shape[2]
    CW = conv_w.shape[2]
    SCALE = float(HD) ** -0.5
    AW = H * HD
    LASTB = T - P
    assert T == NCH * CH and CH <= 512 and KT == 8 and HD == 64 and WB == P and G == 4 and CW == 4 * P

    C_Q, C_K, C_V = 0, AW, AW + P
    C_GA = AW + 2 * P
    C_BG, C_CG, C_HC, C_GC = (C_GA + AW + i * CW for i in range(4))

    A_TILES = [("v", 0, C_V), ("k", 0, C_K)] + [("q", t, C_Q) for t in range(4)]
    for j in range(4):
        A_TILES += [("cg", j, C_CG), ("hc", j, C_HC), ("gc", j, C_GC), ("bg", j, C_BG)]
    A_TILES += [("ga", t, C_GA) for t in range(4)]
    NA = len(A_TILES)
    A_SLOTS, B_SLOTS = NCH * NA, NCH * KT
    GROUPS = A_SLOTS + B_SLOTS + 2 * B_SLOTS
    FT = NA + 2 * KT

    BCAST, V_TURN, KC_TURN, SC_TURN, QPACK = (3, 2), 5, 7, 8, 21
    AT0 = 24
    D0 = AT0 + 4 * NB + 2
    TAILS = 67
    P_LOADS, P_TURNS = (1, 4, 6), (2, 4, 6)

    def units_at(slot, split_last=False):
        out = []
        for u in range(2 * NB):
            at = AT0 + 2 * u
            out += [("pv", u)] * (slot == at + 4) + [("turn", u)] * (slot == at + 2)
            out += [("norm", u)] * (slot == at + 1) + [("cur", u), ("scores", u)] * (slot == at)
            out += [("split", u)] * (slot == at - 2)
        for g in range(2):
            at, u = D0 + 4 * g, 2 * NB + g
            out += [("pv", u)] * (slot == at + 4) + [("turn", u)] * (slot == at + 3) + [("norm", u)] * (slot == at + 2)
            out += [("dscores", u)] * (slot == at + 1) + [("dcache", u)] * (slot == at)
        order = ["pv", "turn", "norm", "cur", "split", "dscores", "scores", "dcache"]
        if split_last:
            order = ["pv", "turn", "norm", "dscores", "scores", "split", "dcache"]
            out = [x for x in out if x[0] != "cur"]
        return sorted(out, key=lambda x: order.index(x[0]))

    def loads_of(w):
        f = w % FT
        if f < NA:
            return 2 if A_TILES[f][0] in ("q", "ga") else 1
        return 3 if f < NA + KT else 2

    def loaded_count(w):
        return 16 * sum(loads_of(i) for i in range(w % 2, w + 1, 2))

    def last_group(w):
        l, f = divmod(w, FT)
        if f < NA + KT:
            return l * GROUPS + NCH * f + NCH - 1
        return l * GROUPS + A_SLOTS + B_SLOTS + 2 * (NCH * (f - NA - KT) + NCH) - 1

    def uses(bank, g):
        return (g + 3 - bank) // 4

    def gates(l, kind, j, c):
        return l * B_SLOTS + (0 if kind == "gc" else 4 * NCH) + NCH * j + c + 1

    def exps(l, u):
        return l * (10 * NB + 4) + (5 * (u + 1) if u < 2 * NB else 10 * NB + 2 * (u + 1 - 2 * NB))

    NSQ = B_SLOTS - NCH
    NTAIL = 5 + 2 * DS
    CONSTS = 16 * (1 + DEPTH * 4)

    with ExitStack() as ctx:
        at = [nc.sbuf_base + (-nc.sbuf_base) % 32]

        def place(name, shape, dtype, offset=None):
            n = 4
            for s in shape[1:]:
                n *= s
            if offset is None:
                offset = at[0]
                at[0] += n + (-n) % 32
            return nc.alloc_sbuf_tensor_at(name, shape, dtype, offset=offset), offset

        act, raw, rot, qps, side, kcT, vc = [], [], [], [], [], [], []
        for i in range(2):
            a, off = place(f"act{i}", [P, 2, KT, T], F32R)
            lo = off + KT * T * 4
            act.append(a)
            raw.append(place(f"raw{i}", [P, 4, T], F32, off)[0])
            rot.append(place(f"rot{i}", [P, T], F32, lo)[0])
            qps.append(place(f"qp{i}", [P, DB, G, DS], F32, lo)[0])
            side.append(place(f"side{i}", [P, DB, P], F32, lo + 4 * T)[0])
            kcT.append(place(f"kcT{i}", [P, DB, P], F32, lo + 4 * T + 4096)[0])
            vc.append(place(f"vc{i}", [P, DB, P], F32, lo + 4 * T + 8192)[0])
            if i == 0:
                xfin, _ = place("xfin", [P, KT, T], F32, off)
            else:
                xnat, _ = place("xnat", [P, NB + 1, D], F32, off)
        stage, _ = place("stage", [P, 2, KT + KP, P], F32)
        ws, _ = place("ws", [P, 2, 2, KT + KP, P], F32R)
        kT, off = place("kT", [P, T], F32)
        vnat, _ = place("vnat", [P, NB + 1, P], F32)
        cosT, cos_at = place("cosT", [P, T], F32)
        sinT, _ = place("sinT", [P, T], F32)
        qst, _ = place("qst", [P, 2, G, P], F32R, cos_at)
        kst, _ = place("kst", [P, 2, 2, 2 * P], F32R, cos_at + 2 * G * P * 4)
        pT, _ = place("pT", [P, 2, KP, T], F32R, off)
        rb, _ = place("rb", [P, T], F32)
        up, off = place("up", [P, 2 + SEQ], F32)
        us, _ = place("us", [P, DB, 2 + DS], F32)
        acc, _ = place("acc", [P, T], F32, off)
        yc, off = place("yc", [P, (NB + 1) * P], F32)
        diag, _ = place("diag", [P, NB + 1, P], F32, off)
        tmp, _ = place("tmp", [P, 2, CH], F32)
        gate, _ = place("gate", [P, 2, CH], F32)
        comb, _ = place("comb", [P, 4, P], F32)
        ptcp, _ = place("ptcp", [P, 2, 4 * P], F32)
        prev_mask, _ = place("prev_mask", [P, P], F32)
        cur_maskT, _ = place("cur_maskT", [P, P], F32)
        ident, _ = place("ident", [P, P], F32)
        ones, _ = place("ones", [P, P], F32)
        dmask, _ = place("dmask", [P, P + NS + G], F32)
        scT, _ = place("scT", [P, 4, 2 * DB], F32)
        utail, _ = place("utail", [P, 4, 2 + NS], F32)
        gT, _ = place("gT", [P, DEPTH + 1, KT], F32)
        cwT, _ = place("cwT", [P, DEPTH, 3, 4], F32)
        sink, _ = place("sink", [P, DEPTH, H], F32)
        sinkd, _ = place("sinkd", [P, DEPTH, 2], F32)
        nsink, _ = place("nsink", [P, DEPTH, H + 2], F32)
        st, _ = place("st", [P, 8, 4], F32)
        nr, _ = place("nr", [P, 7, NB + 1], F32)
        neg, _ = place("neg", [P, 1], F32)
        skt = ptcp[:, 1, 0:P]
        ytmp = yc[:, 0:T].rearrange("p (c n) -> p c n", c=NCH)
        pn = ptcp[:].rearrange("p a n -> p (a n)").rearrange("p (b n) -> p b n", b=4)

        def psum(name, shape):
            return ctx.enter_context(nc.psum_tensor(name, shape, F32))

        ring = psum("ring", [P, 4, 512])
        aux = psum("aux", [P, 4, 512])
        pS = aux[:, 0:2, :].rearrange("p a n -> p (a n)")
        pT1 = aux[:, 2, :]
        pO = aux[:, 3, :]
        x_turns = [aux[:, 0:2, :], aux[:, 2:4, :], ring[:, 2:4, :]]
        y_turns = [pS] + [ring[:, i:i + 2, :].rearrange("p a n -> p (a n)") for i in (0, 2)]
        FIRST = 5
        pS4 = pS.rearrange("p (h n) -> p h n", h=4)

        names = """const_made g_in consts_in x_turned x_hi x_sq x_lo
            loaded0 loaded1 w_scaled w_hi w_lo group_done free0 free1 free2 free3
            ss_done mean_done root_done r_done diag_done bcast_done rb_done
            rot_in roped tables_in v_turned v_taken kc_in kc_turned kc_taken sc_in sc_turned sc_taken
            vc_in q_packed cur_taken qk_hi qk_lo scores_done scores_taken negm_done exp_done probs_ready
            p_turned pt_taken pv_done o_taken dcache_done dcache_taken
            gate_out sum_ready hi_out mix_split mid_split out_split sq_out acc_done
            tail_ready tail_turned tail_taken tail_out p_in p_turned2 p_hi p_lo
            gf_in y_scaled y_turned y_ready0 y_ready1 y_out cache_out dve_step pool_step""".split()
        S = {n: ctx.enter_context(nc.semaphore(n)) for n in names}
        const_made, consts_in = S["const_made"], S["consts_in"]
        loaded = [S["loaded0"], S["loaded1"]]
        free = [S[f"free{i}"] for i in range(4)]
        y_ready = [S["y_ready0"], S["y_ready1"]]
        x_in = [ctx.enter_context(nc.semaphore(f"x_in{b}")) for b in range(NB + 1)]
        group_done, w_hi, w_lo, w_scaled = (S[n] for n in ("group_done", "w_hi", "w_lo", "w_scaled"))

        def cols(c):
            return slice(c * CH, (c + 1) * CH)

        def xblock(b):
            return (b * P, P) if b < NB else (SEQ, NS)

        block = ctx.enter_context(nc.Block())

        @block.sync
        def _(sp):
            for l in range(DEPTH):
                for f in range(FT):
                    w = l * FT + f
                    s = w % 2
                    if w == 1:
                        for b in range(0, NB, 2):
                            sp.dma_start(xnat[:, b, :], x_prompt[0, b * P:(b + 1) * P, :]).then_inc(x_in[b], 16)
                        sp.dma_start(xnat[P - NS:P, NB, :], x_sample.rearrange("b s d -> (b s) d")).then_inc(x_in[NB], 16)
                    if w >= 2:
                        sp.wait_ge(w_lo, w - 1)
                        sp.wait_ge(w_hi, w - 1)
                    if f < NA:
                        kind, j, c0 = A_TILES[f]
                        src = w_in[l].rearrange("(k p) n -> p k n", p=P)
                        if kind in ("q", "ga"):
                            for i in range(2):
                                c = c0 + (j + 4 * i) * HD
                                sp.dma_start(stage[:, s, 0:KT, i * HD:(i + 1) * HD],
                                             src[:, :, c:c + HD]).then_inc(loaded[s], 16)
                        else:
                            c = c0 + j * P
                            sp.dma_start(stage[:, s, 0:KT, :], src[:, :, c:c + P]).then_inc(loaded[s], 16)
                    elif f < NA + KT:
                        c = (f - NA) * P
                        for i in range(2):
                            sp.dma_start(stage[i * HD:(i + 1) * HD, s, 0:4, :],
                                         w_out[l, i * 4 * HD:(i + 1) * 4 * HD, c:c + P]
                                         .rearrange("(t p) n -> p t n", p=HD)).then_inc(loaded[s], 16)
                        sp.dma_start(stage[:, s, 4:8, :], w_out[l, AW:D, c:c + P]
                                     .rearrange("(t p) n -> p t n", p=P)).then_inc(loaded[s], 16)
                    else:
                        c = (f - NA - KT) * P
                        sp.dma_start(stage[:, s, 0:KT, :], w_pg[l, :, c:c + P]
                                     .rearrange("(t p) n -> p t n", p=P)).then_inc(loaded[s], 16)
                        sp.dma_start(stage[:, s, KT:KT + KP, :], w_pp[l, :, c:c + P]
                                     .rearrange("(t p) n -> p t n", p=P)).then_inc(loaded[s], 16)
                    if w == 2:
                        with nc.allow_non_contiguous_dma("a few small vectors, one value to a partition"):
                            for i in range(DEPTH):
                                for r in range(3):
                                    sp.dma_start(cwT[:, i, r, :], conv_w[i, r].rearrange("(k p) -> p k", p=P))\
                                      .then_inc(consts_in, 16)
                                sp.dma_start(sink[:, i, :], sinks[i:i + 1, :].to_broadcast([P, H])).then_inc(consts_in, 16)
                            sp.dma_start(dmask[:], decode_mask).then_inc(consts_in, 16)
                            sp.dma_start(gT[:, DEPTH, :], g_final.rearrange("(k p) -> p k", p=P)).then_inc(S["gf_in"], 16)
                    if f == (1 if l else 2):
                        if l == 0:
                            sp.wait_ge(S["x_turned"], NB + 1)
                        else:
                            sp.wait_ge(group_done, l * GROUPS)
                            sp.wait_ge(S["tail_out"], 16 * NTAIL * l)
                        mx = 1 - l % 2
                        sp.dma_start(cosT[:], rope_cos).then_inc(S["tables_in"], 16)
                        sp.dma_start(sinT[:], rope_sin).then_inc(S["tables_in"], 16)
                        sp.dma_start(comb[0:2 * DB, :, :].rearrange("p a n -> p (a n)"),
                                     state_conv[l].rearrange("b r n -> (b r) n")).then_inc(S["sc_in"], 16)
                        sp.dma_start(side[mx][:], cache_k[l].rearrange("b k g d -> k b (g d)")).then_inc(S["kc_in"], 16)
                        sp.dma_start(vc[mx][:], cache_v[l].rearrange("b k g d -> k b (g d)")).then_inc(S["vc_in"], 16)
                        for new, old in ((new_k_sample, cache_k), (new_v_sample, cache_v)):
                            sp.dma_start(new[l, :, 0:WB - DS].rearrange("b k g d -> b (k g d)"),
                                         old[l, :, DS:WB].rearrange("b k g d -> b (k g d)")).then_inc(S["cache_out"], 16)
                    if f - NA in P_LOADS:
                        i = P_LOADS.index(f - NA)
                        if i == 0:
                            sp.wait_ge(S["tail_out"], 16 * NTAIL * (l + 1))
                            sp.wait_ge(S["pt_taken"], 2 * (2 * NB + 2) * (l + 1))
                            sp.wait_ge(S["pv_done"], (2 * NB + 2) * (l + 1))
                        else:
                            sp.wait_ge(S["p_turned2"], 3 * l + i)
                        if i < 2:
                            sp.dma_start(pn[:], p_prompt[l, 0, i * 4 * P:(i + 1) * 4 * P, :]
                                         .rearrange("(b p) n -> p b n", p=P)).then_inc(S["p_in"], 16)
                        else:
                            sp.dma_start(pn[0:NS, 0, :], p_sample[l].rearrange("b s n -> (b s) n"))\
                              .then_inc(S["p_in"], 16)
            for b in range(NB + 1):
                sp.wait_ge(y_ready[b % 2], b // 2 + 1)
                if b < NB:
                    sp.dma_start(y_prompt[0, b * P:(b + 1) * P, :], xnat[:, b, :]).then_inc(S["y_out"], 16)
                else:
                    sp.dma_start(y_sample.rearrange("b s d -> (b s) d"), xnat[P - NS:P, b, :]).then_inc(S["y_out"], 16)
            sp.wait_ge(S["y_out"], 16 * (NB + 1))
            sp.wait_ge(S["cache_out"], 16 * 2 * DEPTH)
            sp.wait_ge(S["tail_out"], 16 * NTAIL * DEPTH)

        @block.gpsimd
        def _(pool):
            pool.memset(ident[:], 0.0).then_inc(S["pool_step"], 1)
            pool.memset(prev_mask[:], 1.0).then_inc(S["pool_step"], 1)
            pool.memset(cur_maskT[:], 1.0).then_inc(S["pool_step"], 1)
            pool.wait_ge(S["pool_step"], 3)
            pool.affine_select(out=ident[:], in_=ident[:], compare_op=ALU.not_equal, fill=1.0, base=0,
                               pattern=[[-1, P]], channel_multiplier=1).then_inc(const_made, 1)
            pool.affine_select(out=prev_mask[:], in_=prev_mask[:], compare_op=ALU.is_gt, fill=0.0, base=0,
                               pattern=[[1, P]], channel_multiplier=-1).then_inc(const_made, 1)
            pool.affine_select(out=cur_maskT[:], in_=cur_maskT[:], compare_op=ALU.is_ge, fill=0.0, base=0,
                               pattern=[[1, P]], channel_multiplier=-1).then_inc(const_made, 1)
            pool.memset(ones[:], 1.0).then_inc(const_made, 1)
            pool.memset(neg[:], NEG).then_inc(const_made, 1)
            pool.memset(nr[:, 6, NB:NB + 1], 1.0).then_inc(const_made, 1)
            pool.wait_ge(S["g_in"], 16)

            def low_weights(l, first, tiles):
                n = KT if first < NA + KT else KT + KP
                assert first % 2 == 0 and len({loads_of(first + t) for t in range(tiles)}) == 1
                with pool.Fori(0, tiles // 2) as i:
                    for s in range(2):
                        w0 = l * FT + first + s
                        before = loaded_count(w0 - 2) if w0 >= 2 else 0
                        pool.wait_ge(loaded[s], before + 16 * loads_of(w0) * (i + 1))
                        if first < NA:
                            nc.gpsimd.tensor_tensor(stage[:, s, 0:n, :], stage[:, s, 0:n, :],
                                                    gT[:, l, :].rearrange("p (k a) -> p k a", a=1).to_broadcast([P, n, P]),
                                                    ALU.mult).then_inc(w_scaled, 1)
                        pool.wait_ge(w_hi, w0 + 2 * i + 1)
                        nc.gpsimd.tensor_tensor(ws[:, s, 1, 0:n, :], stage[:, s, 0:n, :],
                                                ws[:, s, 0, 0:n, :].bitcast(F32), ALU.subtract).then_inc(w_lo, 1)

            for l in range(DEPTH):
                low_weights(l, 0, 2)
                low_weights(l, 2, 4)
                low_weights(l, 6, 16)
                low_weights(l, 22, 4)
                low_weights(l, NA, KT)
                low_weights(l, NA + KT, KT)

        @block.tensor
        def _(pe):
            def group(g, w, x, tiles, cs, waits=None, turns=0):
                out = ring[:, g % 4, 0:CH]
                if g >= 4:
                    pe.wait_ge(free[g % 4], g // 4 + turns)
                n = len(tiles)
                for i, (kw, kx) in enumerate(tiles):
                    if waits:
                        pe.wait_ge(*waits(i))
                    for wp, xp in ((0, 0), (0, 1), (1, 0)):
                        mm = nc.tensor.matmul(out, ws[:, w % 2, wp, kw, :], x[:, xp, kx, cs],
                                              start=(i == 0 and wp == 0 and xp == 0), stop=(i == n - 1 and wp == 1))
                mm.then_inc(group_done, 1)

            def attention(l, step, u):
                b, g = u // 2, u % 2
                mx = 1 - l % 2
                U = l * (2 * NB + 2) + u
                rows = slice(g * HD, (g + 1) * HD)
                qp = qps[mx]
                if step == "scores":
                    if u == 0:
                        pe.wait_ge(S["roped"], 5 * (l + 1))
                        pe.wait_ge(S["kc_taken"], l + 1)
                        pe.wait_ge(S["sc_taken"], l + 1)
                    else:
                        pe.wait_ge(S["scores_taken"], U)
                    n = l * 2 * NB + u + 1
                    pe.wait_ge(S["qk_hi"], 3 * n)
                    pe.wait_ge(S["qk_lo"], 3 * n)
                    keys = slice(0, P if b == 0 else 2 * P)
                    for t in range(G):
                        for part in range(2):
                            mm = nc.tensor.matmul(pS4[:, t, keys], qst[:, g, t, :], kst[:, g, part, keys],
                                                  start=(part == 0), stop=(part == 1))
                    mm.then_inc(S["scores_done"], 1)
                elif step == "dcache":
                    pe.wait_ge(S["q_packed"], l + 1)
                    pe.wait_ge(S["scores_taken"], U)
                    for i in range(DB):
                        mm = nc.tensor.matmul(pS[:, i * G * DS:(i + 1) * G * DS], kcT[mx][rows, i, :],
                                              qp[rows, i, :, :].rearrange("p a b -> p (a b)"), start=True, stop=True)
                    mm.then_inc(S["dcache_done"], 1)
                elif step == "dscores":
                    pe.wait_ge(S["dcache_taken"], 2 * l + g + 1)
                    nc.tensor.transpose(pS[:, 512:512 + P], skt, ident[:])
                    mm = nc.tensor.matmul(pS[:, 512 + P:512 + P + NS], qp[rows].rearrange("p a b c -> p (a b c)"),
                                          kT[rows, SEQ:T], start=True, stop=True)
                    mm.then_inc(S["scores_done"], 1)
                elif step == "turn":
                    pe.wait_ge(S["probs_ready"], U + 1)
                    if b < NB:
                        for t in range(4):
                            mm = nc.tensor.transpose(pT1[:, t * P:(t + 1) * P], comb[:, t, :], ident[:])
                    else:
                        flat = comb[:].rearrange("p a n -> p (a n)")
                        nc.tensor.transpose(pT1[:, 0:P], flat[:, 0:P], ident[:])
                        mm = nc.tensor.transpose(pT1[0:NS, P:2 * P], flat[:, P:P + NS], ident[:])
                    mm.then_inc(S["p_turned"], 1)
                elif step == "pv":
                    pe.wait_ge(S["pt_taken"], 2 * (U + 1))
                    if g == 0 and b > 0:
                        pe.wait_ge(S["o_taken"], l * (NB + 1) + b)
                    if b < NB:
                        mm = nc.tensor.matmul(pO[rows, :], vnat[:, b, rows], ptcp[:, 0, :], start=True, stop=(b == 0))
                        if b:
                            mm = nc.tensor.matmul(pO[rows, :], vnat[:, b - 1, rows], ptcp[:, 1, :], start=False, stop=True)
                    else:
                        pe.wait_ge(S["vc_in"], 16 * (l + 1))
                        nc.tensor.matmul(pO[rows, 0:P], vnat[0:NS, NB, rows], ptcp[0:NS, 1, 0:P], start=True, stop=False,
                                         skip_group_check=True)
                        for i in range(DB):
                            r = slice(i * G * DS, (i + 1) * G * DS)
                            mm = nc.tensor.matmul(pO[rows, r], vc[mx][:, i, rows], ptcp[:, 0, r], start=False,
                                                  stop=(i == DB - 1), skip_group_check=True)
                    mm.then_inc(S["pv_done"], 1)

            def norm_sums(acc_ready, out=pT1, blocks=range(NB + 1)):
                pe.wait_ge(S["acc_done"], acc_ready)
                for b in blocks:
                    t0 = b * P if b < NB else LASTB
                    mm = nc.tensor.matmul(out[:, b:b + 1], acc[:, t0:t0 + P], ones[:, 0:1], start=True, stop=True)
                mm.then_inc(S["ss_done"], 1)

            def broadcast(l):
                pe.wait_ge(S["diag_done"], l + 1)
                for b in range(NB):
                    mm = nc.tensor.matmul(pS[:, b * P:(b + 1) * P], ones[:], diag[:, b, :], start=True, stop=True)
                    if b == 3:
                        mm.then_inc(S["bcast_done"], 1)
                mm = nc.tensor.matmul(pO[:, 0:P], ones[:], diag[:, NB, :], start=True, stop=True)
                mm.then_inc(S["bcast_done"], 1)

            def turn_x(b):
                n = xblock(b)[1]
                pe.wait_ge(x_in[b], 16)
                if b >= 3:
                    pe.wait_ge(S["x_lo"], b - 2)
                for k in range(KT):
                    mm = nc.tensor.transpose(x_turns[b % 3][:, k // 4, (k % 4) * P:(k % 4) * P + n],
                                             xnat[P - n:P, b, k * P:(k + 1) * P], ident[P - n:P, P - n:P])
                mm.then_inc(S["x_turned"], 1)

            pe.wait_ge(const_made, 6)
            for l in range(DEPTH):
                xa, mx = act[l % 2], act[1 - l % 2]
                m = 1 - l % 2
                g0 = l * GROUPS
                for f in range(NA):
                    w = l * FT + f
                    for c in range(NCH):
                        s = NCH * f + c
                        if l == 0 and f == 0:
                            for b in range(3 * c + 3 if c else 0, min(3 * c + 6, NB + 1)):
                                turn_x(b)
                            pe.wait_ge(S["x_lo"], 3 * c + 3)
                        pe.wait_ge(w_lo, w + 1)
                        waits = None
                        if l and f == 0:
                            waits = lambda i, c=c: (S["out_split"], (l - 1) * B_SLOTS + NCH * i + c + 1)
                        group(g0 + s, w, xa, [(k, k) for k in range(KT)], cols(c), waits)
                        if s == 0 and l:
                            norm_sums(l * NSQ)
                        if s == BCAST[min(l, 1)]:
                            broadcast(l)
                        if s == V_TURN:
                            for g in range(g0, g0 + NCH):
                                pe.wait_ge(free[g % 4], uses(g % 4, g + 1))
                            pe.wait_ge(S["rb_done"], 3 * (l + 1))
                            for b in range(NB):
                                nc.tensor.transpose(pS[:, b * P:(b + 1) * P], rot[m][:, b * P:(b + 1) * P], ident[:])
                            mm = nc.tensor.transpose(pO[0:NS, 0:P], rot[m][:, SEQ:T], ident[:])
                            mm.then_inc(S["v_turned"], 1)
                        if s == KC_TURN:
                            pe.wait_ge(S["kc_in"], 16 * (l + 1))
                            pe.wait_ge(S["v_taken"], 2 * (l + 1))
                            for b in range(DB):
                                mm = nc.tensor.transpose(pS[:, b * P:(b + 1) * P], side[m][:, b, :], ident[:])
                            mm.then_inc(S["kc_turned"], 1)
                        if s == SC_TURN:
                            pe.wait_ge(S["sc_in"], 16 * (l + 1))
                            for j in range(4):
                                mm = nc.tensor.transpose(pO[:, j * 2 * DB:(j + 1) * 2 * DB], comb[0:2 * DB, j, :],
                                                         ident[0:2 * DB, 0:2 * DB])
                            mm.then_inc(S["sc_turned"], 1)
                        for step, u in units_at(s):
                            attention(l, step, u)
                        if s == TAILS:
                            pe.wait_ge(S["tail_ready"], 4 * (l + 1))
                            pe.wait_ge(S["scores_taken"], (2 * NB + 2) * (l + 1))
                            for j in range(4):
                                nc.tensor.transpose(pS[0:2 + NS, j * P:(j + 1) * P], utail[:, j, :], ident[:])
                            nc.tensor.transpose(pS[:, 512:512 + P], kT[:, SEQ - P:SEQ], ident[:])
                            mm = nc.tensor.transpose(pS[0:NS, 640:640 + P], kT[:, SEQ:T], ident[:])
                            mm.then_inc(S["tail_turned"], 1)
                g0 += A_SLOTS
                for f in range(KT):
                    w = l * FT + NA + f
                    pe.wait_ge(w_lo, w + 1)
                    for c in range(NCH):
                        waits = None
                        if f == 0:
                            waits = lambda i, c=c: (S["mix_split"], l * B_SLOTS + NCH * i + c + 1)
                        group(g0 + NCH * f + c, w, mx, [(k, k) for k in (4, 5, 6, 7, 0, 1, 2, 3)], cols(c), waits)
                        if c == 0 and f in P_TURNS:
                            i = P_TURNS.index(f)
                            pe.wait_ge(S["p_in"], 16 * (3 * l + i + 1))
                            if i == 0:
                                pe.wait_ge(S["tail_taken"], 3 * (l + 1))
                            else:
                                pe.wait_ge(S["p_hi"], 3 * l + i)
                                pe.wait_ge(S["p_lo"], 3 * l + i)
                            for k in range(KP):
                                for b in range(4 if i < 2 else 1):
                                    n = P if i < 2 else NS
                                    mm = nc.tensor.transpose(pS[:, k * 512 + b * P:k * 512 + b * P + n],
                                                             pn[0:n, b, k * P:(k + 1) * P], ident[0:n, 0:n])
                            mm.then_inc(S["p_turned2"], 1)
                g0 += B_SLOTS
                pe.wait_ge(S["p_hi"], 3 * (l + 1))
                pe.wait_ge(S["p_lo"], 3 * (l + 1))

                def embedding(f, i=0):
                    w = l * FT + NA + KT + f
                    pe.wait_ge(w_lo, w + 2 * i + 1)
                    turns = 2 * NCH * 2 // 4 * i
                    for c in range(NCH):
                        g = g0 + 2 * (NCH * f + c)
                        group(g, w, pT, [(KT + k, k) for k in range(KP)], cols(c), turns=turns)
                        waits = None
                        if f == 0:
                            waits = lambda k, c=c: (S["mid_split"], l * B_SLOTS + NCH * k + c + 1)
                        group(g + 1, w, xa, [(k, k) for k in range(KT)], cols(c), waits, turns=turns)

                embedding(0)
                embedding(1)
                with pe.Fori(0, KT // 2 - 1) as i:
                    embedding(2, i)
                    embedding(3, i)

            def turn_y(b):
                t0 = b * P if b < NB else LASTB
                if b < 3:
                    pe.wait_ge(S["y_scaled"], B_SLOTS - (b < 2))
                    for i in () if b == 0 else (2 * b - 2, 2 * b - 1):
                        pe.wait_ge(free[i], uses(i, DEPTH * GROUPS))
                else:
                    pe.wait_ge(y_ready[(b - 3) % 2], (b - 3) // 2 + 1)
                for k in range(KT):
                    mm = nc.tensor.transpose(y_turns[b % 3][:, k * P:(k + 1) * P], xfin[:, k, t0:t0 + P], ident[:])
                mm.then_inc(S["y_turned"], 1)

            norm_sums(DEPTH * NSQ - 1, pT1, range(FIRST))
            turn_y(0)
            turn_y(1)
            norm_sums(DEPTH * NSQ, pO, range(FIRST, NB + 1))
            for b in range(2, NB + 1):
                turn_y(b)

        @block.scalar
        def _(sc):
            def split_weights(w):
                f = w % FT
                n = KT if f < NA + KT else KT + KP
                if f < NA:
                    sc.wait_ge(w_scaled, (w // FT) * NA + f + 1)
                else:
                    sc.wait_ge(loaded[w % 2], loaded_count(w))
                if w >= 2:
                    sc.wait_ge(group_done, last_group(w - 2) + 1)
                    sc.wait_ge(w_lo, w - 1)
                nc.scalar.activation(ws[:, w % 2, 0, 0:n, :], stage[:, w % 2, 0:n, :], ACT.Copy).then_inc(w_hi, 1)

            def bank(g):
                sc.wait_ge(group_done, g + 1)
                return ring[:, g % 4, 0:CH]

            def high(dst, s, ready):
                sc.wait_ge(*ready)
                nc.scalar.activation(dst, tmp[:, s % 2, :], ACT.Copy).then_inc(S["hi_out"], 1)

            with nc.allow_non_contiguous_dma("a few small vectors, one value to a partition"):
                sc.dma_start(gT[:, 0:DEPTH, :], g_norm.rearrange("l (k p) -> p l k", p=P)).then_inc(S["g_in"], 16)
                for b in range(1, NB, 2):
                    sc.dma_start(xnat[:, b, :], x_prompt[0, b * P:(b + 1) * P, :]).then_inc(x_in[b], 16)
            def square_x(b):
                r0 = P - xblock(b)[1]
                if b == NB:
                    sc.wait_ge(const_made, 6)
                if b:
                    sc.wait_ge(S["x_sq"], b)
                nc.scalar.activation(diag[r0:P, 0:KT, :].rearrange("p a n -> p (a n)"), xnat[r0:P, b, :], ACT.Square,
                                     accum_out=nr[r0:P, 6, b:b + 1]).then_inc(S["x_sq"], 1)

            for b in range(NB + 1):
                t0, n = xblock(b)
                sc.wait_ge(S["x_turned"], b + 1)
                src = x_turns[b % 3].rearrange("p a (k n) -> p (a k) n", n=P)[:, :, 0:n]
                nc.scalar.activation(act[0][:, 0, :, t0:t0 + n], src, ACT.Copy).then_inc(S["x_hi"], 1)
                if b == 0:
                    split_weights(0)
                for i in {3: (0,), 4: (1, 2), 5: (3,), 6: (4,), 7: (5,), NB: range(6, NB + 1)}.get(b, ()):
                    square_x(i)
                if b == 6:
                    split_weights(1)

            sums = 0
            for l in range(DEPTH):
                xa, mx = act[l % 2], act[1 - l % 2]
                m = 1 - l % 2
                g0 = l * GROUPS
                for s in range(A_SLOTS):
                    f, c = s // NCH, s % NCH
                    w = l * FT + f
                    kind, j, _ = A_TILES[f]
                    g = g0 + s
                    freed = (free[g % 4], uses(g % 4, g + 1))
                    if c == 0 and w >= 1:
                        split_weights(w + 1)
                    if s and A_TILES[(s - 1) // NCH][0] == "ga":
                        sums += 1
                        high(mx[:, 0, A_TILES[(s - 1) // NCH][1], cols((s - 1) % NCH)], s, (S["sum_ready"], sums))
                    if s == 0:
                        sc.wait_ge(S["mean_done"], l + 1)
                        nc.scalar.activation(nr[:, 1, :], nr[:, 0, :], ACT.Sqrt).then_inc(S["root_done"], 1)
                    if s == BCAST[min(l, 1)]:
                        sc.wait_ge(S["bcast_done"], 2 * l + 1)
                        nc.scalar.activation(rb[:, 0:512], pS[:, 0:512], ACT.Copy).then_inc(S["rb_done"], 1)
                        sc.wait_ge(S["bcast_done"], 2 * l + 2)
                        nc.scalar.activation(rb[:, 512:SEQ], pS[:, 512:SEQ], ACT.Copy).then_inc(S["rb_done"], 1)
                        nc.scalar.activation(rb[:, SEQ:T], pO[:, P - NS:P], ACT.Copy).then_inc(S["rb_done"], 1)
                    if s == V_TURN:
                        sc.wait_ge(S["v_turned"], l + 1)
                        nc.scalar.activation(vnat[:, 0:NB, :], pS.rearrange("p (b n) -> p b n", n=P), ACT.Copy)\
                          .then_inc(S["v_taken"], 1)
                        nc.scalar.activation(vnat[0:NS, NB, :], pO[0:NS, 0:P], ACT.Copy).then_inc(S["v_taken"], 1)
                    if s == KC_TURN:
                        sc.wait_ge(S["kc_turned"], l + 1)
                        nc.scalar.activation(kcT[m][:], pS.rearrange("p (b n) -> p b n", n=P), ACT.Copy)\
                          .then_inc(S["kc_taken"], 1)
                    if s == SC_TURN:
                        sc.wait_ge(S["sc_turned"], l + 1)
                        nc.scalar.activation(scT[:], pO[:, 0:8 * DB].rearrange("p (j n) -> p j n", j=4), ACT.Copy)\
                          .then_inc(S["sc_taken"], 1)
                    if 1 <= f < 6 and c == NCH - 1:
                        i = f - 1
                        for h in range(g - NCH + 1, g + 1):
                            sc.wait_ge(free[h % 4], uses(h % 4, h + 1))
                        if i == 0:
                            sc.wait_ge(S["v_turned"], l + 1)
                        else:
                            sc.wait_ge(S["roped"], 5 * l + i)
                        src = kT[:] if i == 0 else raw[m][:, i - 1, :]
                        for a in range(4):
                            o = a ^ 1
                            sc.dma_start(rot[m][32 * a:32 * a + 32, :], src[32 * o:32 * o + 32, :])\
                              .then_inc(S["rot_in"], 16)
                    if kind in ("gc", "ga"):
                        sc.wait_ge(*freed)
                        nc.scalar.activation(gate[:, s % 2, :], gate[:, s % 2, :], ACT.Silu).then_inc(S["gate_out"], 1)
                    for step, u in units_at(s):
                        b, gg = u // 2, u % 2
                        U = l * (2 * NB + 2) + u
                        own, other = slice(gg * HD, (gg + 1) * HD), slice((1 - gg) * HD, (2 - gg) * HD)
                        if step == "split":
                            if u < 2:
                                sc.wait_ge(S["roped"], 5 * (l + 1))
                            else:
                                sc.wait_ge(S["scores_done"], U - 1)
                            tok = slice(b * P, (b + 1) * P)
                            key = slice(b % 2 * P, (b % 2 + 1) * P)
                            nc.scalar.activation(qst[own, gg, :, :], raw[m][own, :, tok], ACT.Copy).then_inc(S["qk_hi"], 1)
                            nc.scalar.activation(kst[own, gg, 0, key], kT[own, tok], ACT.Copy).then_inc(S["qk_hi"], 1)
                            nc.scalar.activation(kst[other, gg, 0, key], kT[own, tok], ACT.Copy).then_inc(S["qk_hi"], 1)
                        elif step == "cur":
                            sc.wait_ge(S["scores_done"], U + 1)
                            nc.scalar.activation(comb[:], pS4[:, :, b % 2 * P:(b % 2 + 1) * P], ACT.Copy).then_inc(S["cur_taken"], 1)
                        elif step == "dcache":
                            sc.wait_ge(S["dcache_done"], 2 * l + gg + 1)
                            nc.scalar.activation(skt, pS[:, 0:P], ACT.Copy).then_inc(S["dcache_taken"], 1)
                        elif step == "pv" and gg == 1:
                            sc.wait_ge(S["pv_done"], U + 1)
                            if b < NB:
                                nc.scalar.activation(raw[m][:, :, b * P:(b + 1) * P],
                                                     pO.rearrange("p (t n) -> p t n", t=4), ACT.Copy)\
                                  .then_inc(S["o_taken"], 1)
                            else:
                                nc.scalar.activation(raw[m][:, :, SEQ:T].rearrange("p h (b s) -> p b h s", s=DS),
                                                     pO[:, 0:P].rearrange("p (b h s) -> p b h s", h=G, s=DS), ACT.Copy)\
                                  .then_inc(S["o_taken"], 1)
                        if step in ("scores", "dscores"):
                            sc.wait_ge(S["negm_done"], 2 * (U + 1))
                            if b < NB:
                                for t in range(4):
                                    nc.scalar.activation(comb[:, t, :], comb[:, t, :], ACT.Exp, bias=st[:, 1, t:t + 1],
                                                         scale=SCALE, accum_out=st[:, 4, t:t + 1]).then_inc(S["exp_done"], 1)
                                nc.scalar.activation(st[:, 3, :], st[:, 2, :], ACT.Exp).then_inc(S["exp_done"], 1)
                            else:
                                flat = comb[:].rearrange("p a n -> p (a n)")[:, 0:P + NS]
                                nc.scalar.activation(flat, flat, ACT.Exp, bias=st[:, 1, 0:1], scale=SCALE,
                                                     accum_out=st[:, 4, 0:1]).then_inc(S["exp_done"], 1)
                                nc.scalar.activation(st[:, 3, 0:1], st[:, 2, 0:1], ACT.Exp).then_inc(S["exp_done"], 1)
                    if kind == "bg":
                        high(mx[:, 0, 4 + j, cols(c)], s, freed)
                    if s == TAILS:
                        sc.wait_ge(S["tail_turned"], l + 1)
                        ctail = comb[:].rearrange("p a n -> p (a n)")[0:2 + NS, :]
                        nc.scalar.activation(ctail, pS[0:2 + NS, 0:512], ACT.Copy).then_inc(S["tail_taken"], 1)
                        nc.scalar.activation(ptcp[:, 0, 0:P], pS[:, 512:512 + P], ACT.Copy).then_inc(S["tail_taken"], 1)
                        nc.scalar.activation(ptcp[0:NS, 0, P:2 * P], pS[0:NS, 640:640 + P], ACT.Copy)\
                          .then_inc(S["tail_taken"], 1)
                        sc.wait_ge(S["tail_taken"], 3 * (l + 1))
                        out = S["tail_out"]
                        sc.dma_start(new_conv_prompt[l, 0], ctail[0:2, :]).then_inc(out, 16)
                        for r in range(2):
                            o = 2 + DS - 2 + r
                            sc.dma_start(new_conv_sample[l, :, r, :], ctail[o:o + DS * (DB - 1) + 1:DS, :]).then_inc(out, 16)
                        sc.dma_start(new_k_prompt[l, 0].rearrange("k g d -> k (g d)"), ptcp[:, 0, 0:P]).then_inc(out, 16)
                        sc.dma_start(new_v_prompt[l, 0].rearrange("k g d -> k (g d)"), vnat[:, NB - 1, :]).then_inc(out, 16)
                        for r in range(DS):
                            sc.dma_start(new_k_sample[l, :, WB - DS + r].rearrange("b g d -> b (g d)"),
                                         ptcp[r:r + DS * (DB - 1) + 1:DS, 0, P:2 * P]).then_inc(out, 16)
                            sc.dma_start(new_v_sample[l, :, WB - DS + r].rearrange("b g d -> b (g d)"),
                                         vnat[r:r + DS * (DB - 1) + 1:DS, NB, :]).then_inc(out, 16)
                sums += 1
                high(mx[:, 0, 3, cols(NCH - 1)], A_SLOTS, (S["sum_ready"], sums))
                g0 += A_SLOTS
                for s in range(B_SLOTS):
                    f, c = s // NCH, s % NCH
                    if c == 0:
                        split_weights(l * FT + NA + f + 1)
                    sums += 1
                    high(xa[:, 0, f, cols(c)], s, (S["sum_ready"], sums))
                    if c == 0 and f in P_TURNS:
                        i = P_TURNS.index(f)
                        sc.wait_ge(S["p_turned2"], 3 * l + i + 1)
                        t0, n = (i * 512, 512) if i < 2 else (SEQ, NS)
                        if i == 0:
                            sc.wait_ge(S["tail_out"], 16 * NTAIL * (l + 1))
                        nc.scalar.activation(pT[:, 0, :, t0:t0 + n], pS.rearrange("p (k n) -> p k n", k=KP)[:, :, 0:n],
                                             ACT.Copy).then_inc(S["p_hi"], 1)
                g0 += B_SLOTS
                for s in range(B_SLOTS):
                    f, c = s // NCH, s % NCH
                    w = l * FT + NA + KT + f
                    if c == 0 and w + 1 < DEPTH * FT:
                        split_weights(w + 1)
                    g = g0 + 2 * s + 1
                    src = bank(g)
                    if s >= 2:
                        sc.wait_ge(free[(g - 5) % 4], uses((g - 5) % 4, g - 4))
                    nc.scalar.activation(gate[:, s % 2, :], src, ACT.Sigmoid).then_inc(free[g % 4], 1)
                    if l < DEPTH - 1:
                        sums += 1
                        high(mx[:, 0, f, cols(c)], s, (S["sum_ready"], sums))
                        last = tmp[:, s % 2, :]
                    else:
                        sc.wait_ge(S["out_split"], l * B_SLOTS + s + 1)
                        last = xfin[:, f, cols(c)]
                    if s >= 2 * NCH:
                        sc.wait_ge(S["acc_done"], l * NSQ + s - 2 * NCH + 1)
                    nc.scalar.activation(acc[:, cols(c)] if f == 0 else ytmp[:, c, :], last, ACT.Square)\
                      .then_inc(S["sq_out"], 1)
                    if l == DEPTH - 1:
                        if s == 0:
                            sc.wait_ge(S["gf_in"], 16)
                        nc.scalar.activation(last, last, ACT.Copy, scale=gT[:, DEPTH, f:f + 1]).then_inc(S["y_scaled"], 1)
            for part in range(2):
                bs = slice(part * FIRST, FIRST if part == 0 else NB + 1)
                sc.wait_ge(S["mean_done"], DEPTH + 1 + part)
                nc.scalar.activation(nr[:, 1, bs], nr[:, 0, bs], ACT.Sqrt).then_inc(S["root_done"], 1)
            for b in range(1, NB + 1, 2):
                sc.wait_ge(S["y_turned"], b + 1)
                sc.wait_ge(S["r_done"], 1 + (b >= FIRST))
                nc.scalar.activation(xnat[:, b, :], y_turns[b % 3], ACT.Copy, scale=nr[:, 5, b:b + 1])\
                  .then_inc(y_ready[1], 1)

        @block.vector
        def _(ve):
            V = nc.vector
            steps = [0]

            def link(ins):
                steps[0] += 1
                ins.then_inc(S["dve_step"], 1)
                ve.wait_ge(S["dve_step"], steps[0])

            def mean(n, sums, bs=slice(0, NB + 1)):
                V.tensor_scalar(nr[:, 0, bs], sums, 1.0 / D, EPS, ALU.mult, ALU.add).then_inc(S["mean_done"], 1)

            def norm_scale(n, bs=slice(0, NB + 1)):
                ve.wait_ge(S["root_done"], n + 1)
                link(V.reciprocal(nr[:, 2, bs], nr[:, 1, bs]))
                link(V.tensor_tensor(nr[:, 3, bs], nr[:, 2, bs], nr[:, 2, bs], ALU.mult))
                link(V.tensor_tensor(nr[:, 4, bs], nr[:, 3, bs], nr[:, 0, bs], ALU.mult))
                link(V.tensor_scalar(nr[:, 3, bs], nr[:, 4, bs], -0.5, 1.5, ALU.mult, ALU.add))
                last = V.tensor_tensor(nr[:, 5, bs], nr[:, 3, bs], nr[:, 2, bs], ALU.mult)
                if n < DEPTH:
                    link(last)
                else:
                    last.then_inc(S["r_done"], 1)
                    ve.wait_ge(S["r_done"], n - DEPTH + 1)

            def bank(g):
                ve.wait_ge(group_done, g + 1)
                return ring[:, g % 4, 0:CH]

            highs = [0]

            def low(x, t, c, s, done):
                dst, hi = x[:, 1, t, cols(c)], x[:, 0, t, cols(c)]
                highs[0] += 1
                ve.wait_ge(S["hi_out"], highs[0])
                V.tensor_tensor(dst, tmp[:, s % 2, :], hi.bitcast(F32), ALU.subtract).then_inc(done, 1)

            ve.wait_ge(const_made, 6)
            for b in range(NB + 1):
                t0, n = xblock(b)
                ve.wait_ge(S["x_hi"], b + 1)
                src = x_turns[b % 3].rearrange("p a (k n) -> p (a k) n", n=P)[:, :, 0:n]
                V.tensor_tensor(act[0][:, 1, :, t0:t0 + n], src, act[0][:, 0, :, t0:t0 + n].bitcast(F32),
                                ALU.subtract).then_inc(S["x_lo"], 1)

            def add_squares(l, s):
                f, c = s // NCH, s % NCH
                ve.wait_ge(S["sq_out"], l * B_SLOTS + s + 1)
                if f == 0:
                    return
                if f >= 2:
                    ve.wait_ge(S["acc_done"], l * NSQ + s - 2 * NCH + 1)
                V.tensor_tensor(acc[:, cols(c)], acc[:, cols(c)], ytmp[:, c, :], ALU.add).then_inc(S["acc_done"], 1)

            for l in range(DEPTH):
                xa, mx = act[l % 2], act[1 - l % 2]
                m = 1 - l % 2
                g0 = l * GROUPS
                if l:
                    ve.wait_ge(S["ss_done"], l)
                    mean(l, pT1[:, 0:NB + 1])
                else:
                    ve.wait_ge(S["x_sq"], NB + 1)
                    mean(l, nr[:, 6, :])
                norm_scale(l)
                V.tensor_tensor(diag[:], ident[:].rearrange("p (a n) -> p a n", a=1).to_broadcast([P, NB + 1, P]),
                                     nr[:, 5, :].rearrange("p (b a) -> p b a", a=1).to_broadcast([P, NB + 1, P]),
                                     ALU.mult).then_inc(S["diag_done"], 1)
                if l == 0:
                    ve.wait_ge(consts_in, CONSTS)
                    link(V.tensor_scalar(nsink[:, :, 0:H], sink[:], -1.0, None, ALU.mult))
                    pick = st[:, 0:2 * DEPTH, :]
                    link(V.tensor_tensor(pick, sink[:].rearrange("p l (g h) -> p (l g) h", h=G),
                                         dmask[:, P + NS:].rearrange("p (a h) -> p a h", a=1).to_broadcast([P, 2 * DEPTH, G]),
                                         ALU.mult))
                    link(V.tensor_reduce(sinkd[:].rearrange("p l g -> p (l g)"), pick, AX.X, ALU.add))
                    link(V.tensor_scalar(nsink[:, :, H:H + 2], sinkd[:], -1.0, None, ALU.mult))
                link(V.memset(up[:, 0:2], 0.0))

                def behind(s):
                    if s >= 2 and A_TILES[(s - 2) // NCH][0] == "ga":
                        low(mx, A_TILES[(s - 2) // NCH][1], (s - 2) % NCH, s - 1, S["mix_split"])
                    if not s or s > A_SLOTS:
                        return
                    kind, j, _ = A_TILES[(s - 1) // NCH]
                    c = (s - 1) % NCH
                    gt = gate[:, (s - 1) % 2, :]
                    if kind == "bg":
                        low(mx, 4 + j, c, s - 1, S["mix_split"])
                    elif kind == "gc":
                        ve.wait_ge(S["gate_out"], gates(l, kind, j, c))
                        link(V.tensor_tensor(ytmp[:, c, :], ytmp[:, c, :], gt, ALU.mult))
                    elif kind == "ga":
                        ve.wait_ge(S["gate_out"], gates(l, kind, j, c))
                        ve.wait_ge(S["o_taken"], (l + 1) * (NB + 1))
                        V.tensor_tensor(tmp[:, s % 2, :], gt, raw[m][:, j, cols(c)], ALU.mult).then_inc(S["sum_ready"], 1)

                def divide(l, u):
                    n = 1 if u // 2 == NB else 4
                    ve.wait_ge(S["exp_done"], exps(l, u))
                    link(V.tensor_tensor(st[:, 5, 0:n], st[:, 4, 0:n], st[:, 3, 0:n], ALU.add))
                    link(V.reciprocal(st[:, 6, 0:n], st[:, 5, 0:n]))
                    if u // 2 == NB:
                        flat = comb[:].rearrange("p a n -> p (a n)")[:, 0:P + NS]
                        V.tensor_scalar(flat, flat, st[:, 6, 0:1], None, ALU.mult).then_inc(S["probs_ready"], 1)
                    else:
                        V.tensor_tensor(comb[:], comb[:], st[:, 6, :].rearrange("p (a n) -> p a n", n=1)
                                        .to_broadcast([P, 4, P]), ALU.mult).then_inc(S["probs_ready"], 1)

                for s in range(A_SLOTS):
                    f, c = s // NCH, s % NCH
                    kind, j, _ = A_TILES[f]
                    for step, u in units_at(s, split_last=True):
                        if step == "norm":
                            divide(l, u)
                    behind(s)
                    g = g0 + s
                    src = bank(g)
                    r = rb[:, cols(c)]
                    if s < 2:
                        ve.wait_ge(S["rb_done"], 3 * l + (1, 3)[s])
                    fr = free[g % 4]
                    if kind in ("v", "k", "q"):
                        dst = {"v": rot[m][:, cols(c)], "k": kT[:, cols(c)], "q": raw[m][:, j, cols(c)]}[kind]
                        V.tensor_tensor(dst, src, r, ALU.mult).then_inc(fr, 1)
                    elif kind == "cg":
                        V.tensor_tensor(ytmp[:, c, :], src, r, ALU.mult).then_inc(fr, 1)
                    elif kind == "hc":
                        t = tmp[:, s % 2, :]
                        V.tensor_tensor(t, src, r, ALU.mult).then_inc(fr, 1)
                    elif kind == "gc":
                        V.tensor_tensor(gate[:, s % 2, :], src, r, ALU.mult).then_inc(fr, 1)
                    elif kind == "bg":
                        V.tensor_tensor(tmp[:, s % 2, :], src, ytmp[:, c, :], ALU.mult).then_inc(fr, 1)
                    elif kind == "ga":
                        V.tensor_tensor(gate[:, s % 2, :], src, r, ALU.mult).then_inc(fr, 1)
                    if 2 <= f < 7 and c == 1:
                        i = f - 2
                        x = kT[:] if i == 0 else raw[m][:, i - 1, :]
                        ve.wait_ge(S["tables_in"], 32 * (l + 1))
                        ve.wait_ge(S["rot_in"], 64 * (5 * l + i + 1))
                        link(V.tensor_tensor(rot[m][:], rot[m][:], sinT[:], ALU.mult))
                        link(V.tensor_tensor(x, x, cosT[:], ALU.mult))
                        V.tensor_tensor(x, x, rot[m][:], ALU.add).then_inc(S["roped"], 1)
                    if s == QPACK:
                        ve.wait_ge(S["roped"], 5 * (l + 1))
                        V.tensor_copy(qps[m][:], raw[m][:, :, SEQ:T].rearrange("p h (b s) -> p b h s", s=DS))\
                         .then_inc(S["q_packed"], 1)
                    for step, u in units_at(s, split_last=True):
                        b, gg = u // 2, u % 2
                        U = l * (2 * NB + 2) + u
                        dec = b == NB
                        n = 1 if dec else 4
                        flat = comb[:].rearrange("p a n -> p (a n)")[:, 0:P + NS]
                        own, other = slice(gg * HD, (gg + 1) * HD), slice((1 - gg) * HD, (2 - gg) * HD)
                        if step == "split":
                            tok = slice(b * P, (b + 1) * P)
                            key = slice(b % 2 * P, (b % 2 + 1) * P)
                            ve.wait_ge(S["qk_hi"], 3 * (l * 2 * NB + u) + 2)
                            V.tensor_tensor(qst[other, gg, :, :], raw[m][own, :, tok], qst[own, gg, :, :].bitcast(F32),
                                            ALU.subtract).then_inc(S["qk_lo"], 1)
                            for half in (own, other):
                                V.tensor_tensor(kst[half, gg, 1, key], kT[own, tok],
                                                kst[own, gg, 0, key].bitcast(F32), ALU.subtract).then_inc(S["qk_lo"], 1)
                        elif step in ("scores", "dscores"):
                            if dec:
                                ve.wait_ge(S["scores_done"], U + 1)
                                V.tensor_tensor(flat, pS[:, 512:512 + P + NS], dmask[:, 0:P + NS], ALU.add).then_inc(S["scores_taken"], 1)
                                ve.wait_ge(S["scores_taken"], U + 1)
                                link(V.tensor_reduce(st[:, 0, 0:1], flat, AX.X, ALU.max))
                                sk, nsk = sinkd[:, l, gg:gg + 1], nsink[:, l, H + gg:H + gg + 1]
                            else:
                                ve.wait_ge(S["cur_taken"], l * 2 * NB + u + 1)
                                mask = prev_mask[:].bitcast(U32).rearrange("p (a n) -> p a n", a=1).to_broadcast([P, 4, P])
                                data = pS4[:, :, (b + 1) % 2 * P:((b + 1) % 2 + 1) * P] if b else neg[:].rearrange("p (a n) -> p a n", a=1).to_broadcast([P, 4, P])
                                V.copy_predicated(comb[:], mask, data).then_inc(S["scores_taken"], 1)
                                ve.wait_ge(S["scores_taken"], U + 1)
                                link(V.tensor_reduce(st[:, 0, :], comb[:], AX.X, ALU.max))
                                sk, nsk = sink[:, l, gg * G:(gg + 1) * G], nsink[:, l, gg * G:(gg + 1) * G]
                            V.scalar_tensor_tensor(st[:, 1, 0:n], st[:, 0, 0:n], -SCALE, nsk, ALU.mult, ALU.min)\
                             .then_inc(S["negm_done"], 1)
                            ve.wait_ge(S["negm_done"], 2 * U + 1)
                            V.tensor_tensor(st[:, 2, 0:n], st[:, 1, 0:n], sk, ALU.add).then_inc(S["negm_done"], 1)
                        elif step == "turn":
                            ve.wait_ge(S["p_turned"], U + 1)
                            if dec:
                                V.tensor_copy(ptcp[:, 0, 0:P], pT1[:, 0:P]).then_inc(S["pt_taken"], 1)
                                V.tensor_copy(ptcp[0:NS, 1, 0:P], pT1[0:NS, P:2 * P]).then_inc(S["pt_taken"], 1)
                            else:
                                pt = pT1.rearrange("p (a n) -> p a n", a=4)
                                V.tensor_tensor(ptcp[:, 0, :].rearrange("p (a n) -> p a n", a=4), pt,
                                                cur_maskT[:].rearrange("p (a n) -> p a n", a=1).to_broadcast([P, 4, P]),
                                                ALU.mult).then_inc(S["pt_taken"], 1)
                                ve.wait_ge(S["pt_taken"], 2 * U + 1)
                                V.tensor_tensor(ptcp[:, 1, :], pT1, ptcp[:, 0, :], ALU.subtract)\
                                 .then_inc(S["pt_taken"], 1)
                    if kind == "hc":
                        ve.wait_ge(fr, uses(g % 4, g + 1))
                        ve.wait_ge(free[(g - NCH) % 4], uses((g - NCH) % 4, g - NCH + 1))
                        n = min(CH, SEQ - c * CH)
                        link(V.tensor_tensor(up[:, 2 + c * CH:2 + c * CH + n], t[:, 0:n], ytmp[:, c, 0:n], ALU.mult))
                        w3 = [cwT[:, l, i, j:j + 1] for i in range(3)]
                        link(V.tensor_scalar(ytmp[:, c, 0:n], up[:, c * CH:c * CH + n], w3[0], None, ALU.mult))
                        for i in (1, 2):
                            link(V.scalar_tensor_tensor(ytmp[:, c, 0:n], up[:, c * CH + i:c * CH + i + n], w3[i],
                                                        ytmp[:, c, 0:n], ALU.mult, ALU.add))
                    if kind == "gc":
                        if c == 0:
                            if j == 0:
                                ve.wait_ge(S["sc_taken"], l + 1)
                            z, n = NCH - 1, SEQ - (NCH - 1) * CH
                            t = tmp[:, (s - 1) % 2, :]
                            w3 = [cwT[:, l, i, j:j + 1] for i in range(3)]
                            link(V.tensor_copy(us[:, :, 0:2], scT[:, j, :].rearrange("p (b r) -> p b r", r=2)))
                            link(V.tensor_tensor(us[:, :, 2:2 + DS], t[:, n:CH].rearrange("p (b s) -> p b s", s=DS),
                                                 ytmp[:, z, n:CH].rearrange("p (b s) -> p b s", s=DS), ALU.mult))
                            ys = ytmp[:, z, n:CH].rearrange("p (b s) -> p b s", s=DS)
                            link(V.tensor_scalar(ys, us[:, :, 0:DS], w3[0], None, ALU.mult))
                            for i in (1, 2):
                                link(V.scalar_tensor_tensor(ys, us[:, :, i:i + DS], w3[i], ys, ALU.mult, ALU.add))
                            link(V.tensor_copy(utail[:, j, 0:2], up[:, SEQ:SEQ + 2]))
                            V.tensor_copy(utail[:, j, 2:2 + NS].rearrange("p (b s) -> p b s", s=DS),
                                          us[:, :, 2:2 + DS]).then_inc(S["tail_ready"], 1)
                        link(V.tensor_tensor(ytmp[:, c, :], ytmp[:, c, :], r, ALU.mult))
                behind(A_SLOTS)
                behind(A_SLOTS + 1)
                ve.wait_ge(S["mix_split"], (l + 1) * B_SLOTS)
                g0 += A_SLOTS
                for s in range(B_SLOTS):
                    f, c = s // NCH, s % NCH
                    if s:
                        low(xa, (s - 1) // NCH, (s - 1) % NCH, s - 1, S["mid_split"])
                    g = g0 + s
                    t = tmp[:, s % 2, :]
                    V.tensor_tensor(t, bank(g), xa[:, 0, f, cols(c)].bitcast(F32), ALU.add).then_inc(free[g % 4], 1)
                    ve.wait_ge(free[g % 4], uses(g % 4, g + 1))
                    V.tensor_tensor(t, t, xa[:, 1, f, cols(c)].bitcast(F32), ALU.add).then_inc(S["sum_ready"], 1)
                    if c == 0 and f in P_TURNS:
                        i = P_TURNS.index(f)
                        ve.wait_ge(S["p_hi"], 3 * l + i + 1)
                        t0, n = (i * 512, 512) if i < 2 else (SEQ, NS)
                        V.tensor_tensor(pT[:, 1, :, t0:t0 + n], pS.rearrange("p (k n) -> p k n", k=KP)[:, :, 0:n],
                                        pT[:, 0, :, t0:t0 + n].bitcast(F32), ALU.subtract).then_inc(S["p_lo"], 1)
                low(xa, KT - 1, NCH - 1, B_SLOTS - 1, S["mid_split"])
                g0 += B_SLOTS
                for s in range(B_SLOTS):
                    f, c = s // NCH, s % NCH
                    if s:
                        if l < DEPTH - 1:
                            low(mx, (s - 1) // NCH, (s - 1) % NCH, s - 1, S["out_split"])
                        add_squares(l, s - 1)
                    g = g0 + 2 * s
                    src = bank(g)
                    t = tmp[:, s % 2, :]
                    ve.wait_ge(free[(g + 1) % 4], uses((g + 1) % 4, g + 2))
                    V.tensor_tensor(t, src, gate[:, s % 2, :], ALU.mult).then_inc(free[g % 4], 1)
                    ve.wait_ge(free[g % 4], uses(g % 4, g + 1))
                    link(V.tensor_tensor(t, t, xa[:, 0, f, cols(c)].bitcast(F32), ALU.add))
                    if l < DEPTH - 1:
                        V.tensor_tensor(t, t, xa[:, 1, f, cols(c)].bitcast(F32), ALU.add).then_inc(S["sum_ready"], 1)
                    else:
                        V.tensor_tensor(xfin[:, f, cols(c)], t, xa[:, 1, f, cols(c)].bitcast(F32), ALU.add)\
                         .then_inc(S["out_split"], 1)
                if l < DEPTH - 1:
                    low(mx, KT - 1, NCH - 1, B_SLOTS - 1, S["out_split"])
                add_squares(l, B_SLOTS - 1)
            def scale_y(b):
                ve.wait_ge(S["y_turned"], b + 1)
                V.tensor_scalar(xnat[:, b, :], y_turns[b % 3], nr[:, 5, b:b + 1], None, ALU.mult).then_inc(y_ready[0], 1)

            first, rest = slice(0, FIRST), slice(FIRST, NB + 1)
            ve.wait_ge(S["ss_done"], DEPTH)
            mean(DEPTH, pT1[:, first], first)
            norm_scale(DEPTH, first)
            ve.wait_ge(S["ss_done"], DEPTH + 1)
            mean(DEPTH + 1, pO[:, rest], rest)
            scale_y(0)
            norm_scale(DEPTH + 1, rest)
            for b in range(2, NB + 1, 2):
                scale_y(b)


_INS = ["x_prompt", "x_sample", "cache_k", "cache_v", "state_conv", "p_prompt", "p_sample", "g_norm", "w_in",
        "sinks", "conv_w", "w_out", "w_pg", "w_pp", "g_final"]


def _constants(seq, batch, steps, past, head_dim, group, window):
    import numpy as np

    inv = (10000.0 ** (-np.arange(0, head_dim, 2) / head_dim)).astype(np.float32)
    pos = np.concatenate([np.arange(seq), np.tile(past + np.arange(steps), batch)]).astype(np.float32)
    ang = (inv[:, None] * pos[None, :]).astype(np.float64)
    cos, sin = np.cos(ang).astype(np.float32), np.sin(ang).astype(np.float32)
    b, h, s = (a.ravel()[:, None] for a in np.indices((batch, group, steps)))
    cached = np.arange(window)[None, :] > s
    kb, ks = (a.ravel()[None, :] for a in np.indices((batch, steps)))
    new = (kb == b) & (ks <= s)
    mask = np.where(np.concatenate([cached, new], 1), 0.0, -1e30)
    flags = np.arange(group)[None, :] == h
    return (np.tile(cos, (4, 1)), np.concatenate([-sin, sin] * 2, 0),
            np.concatenate([mask, flags], 1).astype(np.float32))


def kernel(**inputs):
    import numpy as _np
    import concourse.bacc as _bacc
    from concourse import mybir as _mybir
    from concourse.bass_utils import run_bass_kernel_spmd as _run

    nc = _bacc.Bacc("TRN2", target_bir_lowering=False, num_devices=1)
    arrays, args = {}, []

    def give(name, a):
        arrays[f"in_{name}_dram"] = a
        args.append(nc.dram_tensor(f"in_{name}_dram", a.shape, _mybir.dt.from_np(a.dtype), kind="ExternalInput").ap())

    for name in _INS:
        give(name, _np.ascontiguousarray(inputs[name]))
    shape = {n: inputs[n].shape for n in _INS}
    depth, batch, window, kv, head_dim = shape["cache_k"]
    tables = _constants(shape["x_prompt"][1], batch, shape["x_sample"][1], 4096, head_dim,
                        shape["sinks"][1] // kv, window)
    for name, a in zip(("rope_cos", "rope_sin", "decode_mask"), tables):
        give(name, _np.ascontiguousarray(a))
    f32 = _mybir.dt.float32
    conv = shape["state_conv"]
    outs = [shape["x_prompt"], shape["x_sample"], (depth, 1, window, kv, head_dim), (depth, 1, window, kv, head_dim),
            (depth, 1, conv[2], conv[3]), shape["cache_k"], shape["cache_v"], conv]
    for i, s in enumerate(outs):
        args.append(nc.dram_tensor(f"out_{i}_dram", s, f32, kind="ExternalOutput").ap())
    hybrid_trunk(nc, *args)
    r = _run(nc, [arrays], core_ids=[0])
    return tuple(r.results[0][f"out_{i}_dram"] for i in range(len(outs)))
```
